# Optimizing a Trainium2 kernel written in Bass

```python
import jax, jax.numpy as jnp
from jax import lax
import numpy as np

D_MODEL = 2048
BATCH = 1
SEQ = 256
DEPTH = 1

HEAD_DIM = 128
N_MLSTM_HEADS = D_MODEL // 2 // HEAD_DIM
N_RET_HEADS = D_MODEL // 2 // HEAD_DIM
D_MLSTM = N_MLSTM_HEADS * HEAD_DIM
D_RET = N_RET_HEADS * HEAD_DIM
D_MIX = D_MLSTM + D_RET
D_PROJ = 4 * D_MLSTM + 2 * N_MLSTM_HEADS + 4 * D_RET
CHUNK = 128
CONV_WIDTH = 4
ROPE_BASE = 10000.0
D_FF = -(-(8 * D_MODEL) // (3 * 256)) * 256
NORM_EPS = 1e-6

kernel_name = "hybrid_mlstm_retention_sandwich_block"

SPLITS = list(np.cumsum([D_MLSTM, D_MLSTM, D_MLSTM, D_MLSTM, N_MLSTM_HEADS, N_MLSTM_HEADS, D_RET, D_RET, D_RET]))

def rmsnorm(x, g):
    xf = x.astype(jnp.float32)
    y = xf * lax.rsqrt(jnp.mean(xf * xf, axis=-1, keepdims=True) + NORM_EPS)
    return (y * g.astype(jnp.float32)).astype(x.dtype)

def head_rmsnorm(h, g):
    B, S, H, D = h.shape
    y = h * lax.rsqrt(jnp.mean(h * h, axis=-1, keepdims=True) + NORM_EPS)
    return y.reshape(B, S, H * D) * g.astype(jnp.float32)

def causal_dwconv(u, w, b):
    C = u.shape[-1]
    out = lax.conv_general_dilated(u, w.astype(u.dtype)[:, None, :], window_strides=(1,),
                                   padding=[(CONV_WIDTH - 1, 0)],
                                   dimension_numbers=("NWC", "WIO", "NWC"),
                                   feature_group_count=C)
    return out + b.astype(u.dtype)

def split_heads(t, H):
    B, S, _ = t.shape
    return t.reshape(B, S, H, HEAD_DIM)

def rotary(t, positions):
    D = t.shape[-1]
    inv_freq = ROPE_BASE ** (-jnp.arange(0, D, 2, dtype=jnp.float32) / D)
    ang = positions.astype(jnp.float32)[..., None] * inv_freq
    cos, sin = jnp.cos(ang)[:, :, None, :], jnp.sin(ang)[:, :, None, :]
    t1, t2 = t[..., : D // 2], t[..., D // 2:]
    return jnp.concatenate([t1 * cos - t2 * sin, t2 * cos + t1 * sin], axis=-1)

def to_chunks(t):
    B, S, H, D = t.shape
    return t.reshape(B, S // CHUNK, CHUNK, H, D).transpose(0, 3, 1, 2, 4)

def gate_chunks(t):
    B, S, H = t.shape
    return t.reshape(B, S // CHUNK, CHUNK, H).transpose(0, 3, 1, 2)

def from_chunks(t):
    B, H, NC, L, D = t.shape
    return t.transpose(0, 2, 3, 1, 4).reshape(B, NC * L, H, D)

def mlstm_chunkwise(q, k, v, i_pre, f_pre):
    B, S, H, D = q.shape
    q, k, v = to_chunks(q), to_chunks(k) * (D ** -0.5), to_chunks(v)
    ig = gate_chunks(i_pre)
    b = jnp.cumsum(gate_chunks(jax.nn.log_sigmoid(f_pre)), axis=-1)
    b_last = b[..., -1]
    w_end = b_last[..., None] - b + ig

    def step(carry, inp):
        C, n, m = carry
        kc, vc, wc, bl = inp
        m_new = jnp.maximum(bl + m, wc.max(-1))
        decay = jnp.exp(bl + m - m_new)
        a = jnp.exp(wc - m_new[..., None])[..., None] * kc
        C_new = decay[..., None, None] * C + jnp.einsum("bhld,bhle->bhde", a, vc)
        n_new = decay[..., None] * n + a.sum(axis=2)
        return (C_new, n_new, m_new), (C, n, m)

    init = (jnp.zeros((B, H, D, D), jnp.float32), jnp.zeros((B, H, D), jnp.float32),
            jnp.zeros((B, H), jnp.float32))
    xs = (jnp.moveaxis(k, 2, 0), jnp.moveaxis(v, 2, 0), jnp.moveaxis(w_end, 2, 0), jnp.moveaxis(b_last, 2, 0))
    _, (C0, n0, m0) = lax.scan(step, init, xs)
    C0 = jnp.moveaxis(C0, 0, 2)
    n0 = jnp.moveaxis(n0, 0, 2)
    m0 = jnp.moveaxis(m0, 0, 2)

    causal = jnp.tril(jnp.ones((CHUNK, CHUNK), dtype=bool))
    log_d = jnp.where(causal, b[..., :, None] - b[..., None, :] + ig[..., None, :], -jnp.inf)
    log_inter = b + m0[..., None]
    m_row = jnp.maximum(log_inter, log_d.max(-1))
    dmat = jnp.exp(log_d - m_row[..., None])
    inter_scale = jnp.exp(log_inter - m_row)
    s = jnp.einsum("bhcld,bhcsd->bhcls", q, k) * dmat
    num = inter_scale[..., None] * jnp.einsum("bhcld,bhcde->bhcle", q, C0) + jnp.einsum("bhcls,bhcse->bhcle", s, v)
    den = inter_scale * jnp.einsum("bhcld,bhcd->bhcl", q, n0) + s.sum(-1)
    h = num / jnp.maximum(jnp.abs(den), jnp.exp(-m_row))[..., None]
    return from_chunks(h)

def retention_chunkwise(q, k, v):
    B, S, H, D = q.shape
    log_gamma = jnp.log(1.0 - jnp.exp2(-5.0 - jnp.arange(H, dtype=jnp.float32)))
    q, k, v = to_chunks(q), to_chunks(k) * (D ** -0.5), to_chunks(v)
    idx = jnp.arange(CHUNK, dtype=jnp.float32)
    rel = idx[:, None] - idx[None, :]
    decay_mask = jnp.where(rel >= 0, jnp.exp(log_gamma[:, None, None] * jnp.maximum(rel, 0.0)), 0.0)
    scores = jnp.einsum("bhcld,bhcsd->bhcls", q, k) * decay_mask[None, :, None]
    o_intra = jnp.einsum("bhcls,bhcse->bhcle", scores, v)

    key_decay = jnp.exp(log_gamma[:, None] * (CHUNK - 1 - idx))
    U = jnp.einsum("bhcld,bhcle->bhcde", k * key_decay[None, :, None, :, None], v)
    chunk_decay = jnp.exp(log_gamma * CHUNK)[None, :, None, None]

    def step(R, u):
        return chunk_decay * R + u, R

    _, R0 = lax.scan(step, jnp.zeros((B, H, D, D), jnp.float32), jnp.moveaxis(U, 2, 0))
    R0 = jnp.moveaxis(R0, 0, 2)
    query_decay = jnp.exp(log_gamma[:, None] * (idx + 1.0))
    o_inter = jnp.einsum("bhcld,bhcde->bhcle", q * query_decay[None, :, None, :, None], R0)
    return from_chunks(o_intra + o_inter)

def setup_inputs(seed: int = 0) -> dict:
    key = jax.random.key(seed)
    ks = jax.random.split(key, 20)
    f32 = jnp.float32

    def nrm(k, shape, scale):
        return jax.random.normal(k, shape, f32) * scale

    def gain(k, shape):
        return 1.0 + 0.02 * jax.random.normal(k, shape, f32)

    x = jax.random.normal(ks[0], (BATCH, SEQ, D_MODEL), f32)
    start = jax.random.randint(ks[1], (BATCH, 1), 0, 1024, dtype=jnp.int32)
    positions = (start + jnp.arange(SEQ, dtype=jnp.int32)[None, :]).astype(jnp.int32)
    b_fgate = jnp.linspace(3.0, 6.0, N_MLSTM_HEADS, dtype=f32)[None, :] + nrm(ks[7], (DEPTH, N_MLSTM_HEADS), 0.01)
    return {
        "x": x,
        "positions": positions,
        "g_mix_pre": gain(ks[2], (DEPTH, D_MODEL)),
        "w_in": nrm(ks[3], (DEPTH, D_MODEL, D_PROJ), D_MODEL ** -0.5),
        "conv_w": nrm(ks[4], (DEPTH, CONV_WIDTH, 2 * D_MLSTM), CONV_WIDTH ** -0.5),
        "conv_b": nrm(ks[5], (DEPTH, 2 * D_MLSTM), 0.02),
        "b_igate": nrm(ks[6], (DEPTH, N_MLSTM_HEADS), 0.1),
        "b_fgate": b_fgate,
        "g_mlstm_head": gain(ks[8], (DEPTH, D_MLSTM)),
        "g_ret_head": gain(ks[9], (DEPTH, D_RET)),
        "w_out": nrm(ks[10], (DEPTH, D_MIX, D_MODEL), D_MIX ** -0.5),
        "g_mix_post": gain(ks[11], (DEPTH, D_MODEL)),
        "g_ffn_pre": gain(ks[12], (DEPTH, D_MODEL)),
        "w_gate": nrm(ks[13], (DEPTH, D_MODEL, D_FF), D_MODEL ** -0.5),
        "w_up": nrm(ks[14], (DEPTH, D_MODEL, D_FF), D_MODEL ** -0.5),
        "w_down": nrm(ks[15], (DEPTH, D_FF, D_MODEL), D_FF ** -0.5),
        "g_ffn_post": gain(ks[16], (DEPTH, D_MODEL)),
    }

def reference(x, positions, g_mix_pre, w_in, conv_w, conv_b, b_igate, b_fgate, g_mlstm_head, g_ret_head,
              w_out, g_mix_post, g_ffn_pre, w_gate, w_up, w_down, g_ffn_post):
    f32 = jnp.float32
    for l in range(DEPTH):
        h = rmsnorm(x, g_mix_pre[l])
        proj = h @ w_in[l]
        mq, mk, mv, mo, mi, mf, rq, rk, rv, rg = jnp.split(proj, SPLITS, axis=-1)

        qk = jax.nn.silu(causal_dwconv(jnp.concatenate([mq, mk], axis=-1), conv_w[l], conv_b[l]))
        mq, mk = qk[..., :D_MLSTM], qk[..., D_MLSTM:]
        hm = mlstm_chunkwise(split_heads(mq, N_MLSTM_HEADS).astype(f32),
                             split_heads(mk, N_MLSTM_HEADS).astype(f32),
                             split_heads(mv, N_MLSTM_HEADS).astype(f32),
                             (mi + b_igate[l]).astype(f32), (mf + b_fgate[l]).astype(f32))
        hm = head_rmsnorm(hm, g_mlstm_head[l]) * jax.nn.sigmoid(mo.astype(f32))

        rq_h = rotary(split_heads(rq, N_RET_HEADS).astype(f32), positions)
        rk_h = rotary(split_heads(rk, N_RET_HEADS).astype(f32), positions)
        hr = retention_chunkwise(rq_h, rk_h, split_heads(rv, N_RET_HEADS).astype(f32))
        hr = head_rmsnorm(hr, g_ret_head[l]) * jax.nn.silu(rg.astype(f32))

        mix = jnp.concatenate([hm, hr], axis=-1).astype(x.dtype) @ w_out[l]
        x = x + rmsnorm(mix, g_mix_post[l])

        h = rmsnorm(x, g_ffn_pre[l])
        ff = (jax.nn.silu(h @ w_gate[l]) * (h @ w_up[l])) @ w_down[l]
        x = x + rmsnorm(ff, g_ffn_post[l])
    return x


_drawn_inputs = setup_inputs


def setup_inputs(seed=0):
    import zlib

    import numpy as np

    out = dict(_drawn_inputs(seed))
    spreads = {}
    factors = {'conv_b': 2.695,
     'b_igate': 148.377,
     'g_mlstm_head': 57.431,
     'g_ret_head': 48.551,
     'g_mix_post': 3.541,
     'g_ffn_pre': 3.496,
     'g_ffn_post': 53.543}
    for name, (base, spread) in spreads.items():
        noise = np.random.default_rng([zlib.crc32(name.encode()), seed]).standard_normal(out[name].shape)
        drawn = base * np.exp(spread * noise) if base else spread * noise
        out[name] = __import__('jax').numpy.asarray(drawn.astype(out[name].dtype))
    for name, factor in factors.items():
        out[name] = (out[name] * factor).astype(out[name].dtype)
    return out
```

```python
import math
from contextlib import ExitStack

import numpy as np

import concourse.bass as bass
from concourse import mybir

ALU = mybir.AluOpType
ACT = mybir.ActivationFunctionType
F32 = mybir.dt.float32
F32R = mybir.dt.float32r
I32 = mybir.dt.int32

P = 128
SEQ = 256
D = 2048
HD = 128
HEADS = 8
DH = HEADS * HD
D_FF = 5632
KT = D // P
KF = D_FF // P
TT = SEQ // P
CONV = 4
EPS = 1e-6
SCALE = HD ** -0.5
COL_RET = 4 * DH + 2 * HEADS

SUB = 1024
RAW_CHUNKS = 4
AHEAD = 4
R_V = 0
R_IN = R_V + 4
R_OUT = R_IN + 12
R_FF = R_OUT + 4
PAIRS = D_FF // 256
R_DOWN = R_FF + PAIRS
DOWN_SUBS = KF // 2
N_SUBS = 8 * R_DOWN + 4 * DOWN_SUBS
E_IN = 4
E_OUT = E_IN + 24
E_FF = E_OUT + 4
E_DOWN = E_FF + 2 * PAIRS
C_GPRE, C_GFFN, C_CONVB, C_GHEAD, C_CONVW = 0, 16, 32, 48, 64

TWO_PI_1 = 6.28125
TWO_PI_2 = float(np.float32(np.float64(2 * np.pi - 6.28125).astype(np.float16)))
TWO_PI_3 = float(np.float32(2 * np.pi - 6.28125 - TWO_PI_2))
ROUND = 1.5 * 2.0 ** 23
LOG_GAMMA = [math.log(1.0 - 2.0 ** (-5.0 - h)) for h in range(HEADS)]


S_SQ, S_VAR, S_SD, S_RSTD = 0, 2, 4, 6
S_DEN, S_RECIP, S_HSQ, S_HVAR, S_HSD, S_HRSTD, S_HSCALE = 8, 10, 12, 14, 16, 18, 20
S_PSQ, S_PSUM, S_PVAR, S_PSD, S_PRSTD = 24, 32, 34, 36, 38


def event_of(rnd, unit):
    return 2 * rnd - 4 + unit


def gate_round(group):
    return R_IN + 3 * group + 2


def head_at(rnd, s, first):
    for group in range(4):
        n, odd = divmod(8 * (rnd - gate_round(group)) + s - first, 2)
        if not odd and 0 <= n < 4:
            return 4 * group + n
    return None


def hybrid_layer(nc, x, positions, g_mix_pre, w_in, conv_w, conv_b, b_igate, b_fgate, g_mlstm_head,
                 g_ret_head, w_out, g_mix_post, g_ffn_pre, w_gate, w_up, w_down, g_ffn_post,
                 inv_freq, out):
    with ExitStack() as ctx:
        def sb(name, shape, dt=F32, stack=ctx):
            return stack.enter_context(nc.sbuf_tensor(name, shape, dt))

        def sem(name):
            return ctx.enter_context(nc.semaphore(name))

        raw = sb("raw", [P, RAW_CHUNKS, 2 * SUB])
        w_hi = sb("w_hi", [P, AHEAD, SUB], F32R)
        w_lo = sb("w_lo", [P, AHEAD, SUB], F32R)
        resid = sb("resid", [P, TT, D])
        ident = sb("ident", [P, P])
        coef = sb("coef", [P, P])
        right = sb("right", [P, 2, SEQ])
        stat = sb("stat", [P, 64])

        mixer = ExitStack()
        late = ExitStack()
        mixed = sb("mixed", [P, TT, D], stack=late)
        g_post1 = sb("g_post1", [P, D], stack=late)
        late.close()
        decay = sb("decay", [P, 2 * HEADS, 3 * P], stack=mixer)
        v_sb = sb("v_sb", [P, TT, 2 * HEADS, HD + 1], stack=mixer)
        hT = sb("hT", [P, KT, 2 * SEQ], F32R, stack=mixer)
        start = ExitStack()
        h0 = sb("h0", [P, TT, D], stack=start)
        sel = sb("sel", [HEADS, HEADS, P], stack=start)
        rel = sb("rel", [P, 3 * P], stack=start)
        causal = sb("causal", [P, 2, P], stack=start)
        wg = sb("wg", [P, KT, 40], stack=start)
        wg_hi = sb("wg_hi", [P, KT, 40], F32R, stack=start)
        wg_lo = sb("wg_lo", [P, KT, 40], F32R, stack=start)
        start.close()
        mixT = sb("mixT", [P, KT, 2 * SEQ], F32R, stack=mixer)
        qT = sb("qT", [P, 4, SEQ], stack=mixer)
        kT = sb("kT", [P, 4, SEQ], stack=mixer)
        gT = sb("gT", [P, 4, SEQ], stack=mixer)
        probs = sb("probs", [P, 3 * P], stack=mixer)
        y = sb("y", [P, 2, TT, HD], stack=mixer)
        pre = sb("pre", [P, 2, SEQ + CONV - 1], stack=mixer)
        cosT = sb("cosT", [P, SEQ], stack=mixer)
        sinT = sb("sinT", [P, SEQ], stack=mixer)
        a_col = sb("a_col", [P, TT, HEADS], stack=mixer)
        floor = sb("floor", [P, TT, 2 * HEADS], stack=mixer)
        vec = sb("vec", [P, 4], stack=mixer)
        mixer.close()
        sg = pre[:, :, CONV - 1:]
        spin = gT[:, 0:2, :]
        ffn = ExitStack()
        ffT = sb("ffT", [P, KF, 2 * SEQ], F32R, stack=ffn)
        last = ExitStack()
        ff_out = sb("ff_out", [P, TT, D], stack=last)
        g_post2 = sb("g_post2", [P, D], stack=last)
        last.close()
        h2T = sb("h2T", [P, KT, 2 * SEQ], F32R, stack=ffn)
        ff_g = sb("ff_g", [P, 2, SEQ], stack=ffn)
        ff_u = sb("ff_u", [P, 2, SEQ], stack=ffn)
        ctx.callback(ffn.close)

        def row(n):
            return h0[:, n // 8, (n % 8) * SEQ:(n % 8 + 1) * SEQ]

        R_RIGHT, R_Z, R_ABS, R_EXP, R_LN, R_A, R_F, R_M, R_FLOOR, R_NEGM, R_NEGROW, R_ONES = range(12)
        R_MASKED, R_OPEN = 12, 14

        bank = ctx.enter_context(nc.psum_tensor("bank", [P, 8, 512], F32))
        B_S, B_PV, B_T = 4, 5, 7

        def acc(pair):
            return bank[:, 2 * pair:2 * pair + 2, :]

        def spread(h):
            b = 5 + h // 2 if h < 6 else 4
            return bank[:, b, (h % 2) * SEQ:(h % 2 + 1) * SEQ]

        def pv_out(a):
            return bank[:, B_PV + a % 2, 0:TT * (HD + 1)].rearrange("p (t c) -> p t c", t=TT)

        raw_full = [sem(f"raw_full{n}") for n in range(RAW_CHUNKS)]
        hi_done = sem("hi_done")
        lo_done = sem("lo_done")
        sub_done = sem("sub_done")
        acc_free = sem("acc_free")
        right_ready = sem("right_ready")
        x_in = [sem(f"x_in{t}") for t in range(TT)]
        small_in = sem("small_in")
        wg_in = sem("wg_in")
        post_in = sem("post_in")
        zeroed = sem("zeroed")
        consts = sem("consts")
        dve_step = sem("dve_step")
        sq_done = sem("sq_done")
        var_ready = sem("var_ready")
        sd_ready = sem("sd_ready")
        resid_ready = sem("resid_ready")
        h_ready = sem("h_ready")
        xT_done = sem("xT_done")
        xT_hi = sem("xT_hi")
        xT_lo = sem("xT_lo")
        coef_T = sem("coef_T")
        coef_ready = sem("coef_ready")
        wg_rounded = sem("wg_rounded")
        wg_ready = sem("wg_ready")
        gates_full = sem("gates_full")
        gates_act = sem("gates_act")
        gates_dve = sem("gates_dve")
        cols_T = sem("cols_T")
        cols_ready = sem("cols_ready")
        spread_done = sem("spread_done")
        masked = sem("masked")
        decay_ready = sem("decay_ready")
        angles = sem("angles")
        rope_ready = sem("rope_ready")
        conv_done = sem("conv_done")
        sig_done = sem("sig_done")
        qk_ready = sem("qk_ready")
        scores_done = sem("scores_done")
        probs_ready = sem("probs_ready")
        pv_done = sem("pv_done")
        den_ready = sem("den_ready")
        recip_ready = sem("recip_ready")
        y_ready = sem("y_ready")
        yT_done = sem("yT_done")
        mix_ready = sem("mix_ready")
        mix_hi = sem("mix_hi")
        mix_lo = sem("mix_lo")
        silu_done = sem("silu_done")
        ff_ready = sem("ff_ready")
        ff_hi = sem("ff_hi")
        ff_lo = sem("ff_lo")
        stored = sem("stored")

        SMALL = 16 * 10
        CONSTS = 9
        with_sigmoid = [event_of(r, u) for r in range(R_IN, R_OUT) for u in range(2)
                        if r < gate_round(1) + 1 or (r - R_IN) % 3 == 2]

        def sig_count(event):
            return with_sigmoid.index(event) + 1

        V_HEADS = TT
        V_POST1 = V_HEADS + 2 * HEADS + 1
        V_NORM2 = V_POST1
        V_POST2 = V_NORM2 + TT + 1
        Q_HEADS = TT
        Q_POST1 = Q_HEADS + TT * 2 * HEADS
        Q_NORM2 = Q_POST1 + 4 * TT
        Q_POST2 = Q_NORM2 + TT

        block = ctx.enter_context(nc.Block())

        @block.sync
        def _(sp):
            def load(rnd, q, src, wait=True):
                if wait:
                    sp.wait_ge(lo_done, 8 * (rnd - 1) + 2 * q + 2)
                k = src.shape[1]
                sp.dma_start(raw[:, q, :].rearrange("p (k c) -> p k c", k=k), src)\
                  .then_inc(raw_full[q], 16)

            def rows(w, k0, n, col, width):
                return w[k0 * P:(k0 + n) * P, bass.ds(col, width)].rearrange("(k p) c -> p k c", p=P)

            for t in range(TT):
                sp.dma_start(resid[:, t, :], x[0, t * P:(t + 1) * P, :]).then_inc(x_in[t], 16)
            for r in range(4):
                for q in range(4):
                    col = 2 * DH + (r % 2) * 512 + (r // 2) * COL_RET
                    load(r, q, rows(w_in, 4 * q, 4, col, 512), wait=r > 0)
            with sp.Fori(0, 2) as kind:
                with sp.Fori(0, 2) as half:
                    for n, part in enumerate((0, 1, 3)):
                        for q in range(4):
                            col = COL_RET * kind + 512 * half + (part * DH + (q // 2) * 256)
                            load(6 * kind + 3 * half + (R_IN + n), q,
                                 rows(w_in, 8 * (q % 2), 8, col, 256))
            with sp.Fori(0, 4) as g:
                for q in range(4):
                    load(g + R_OUT, q, rows(w_out, 4 * q, 4, 512 * g, 512))
            with sp.Fori(0, PAIRS) as i:
                for q in range(4):
                    load(i + R_FF, q, rows(w_gate if q < 2 else w_up, 8 * (q % 2), 8, 256 * i, 256))
            for n in range(4 * KF // 4):
                g, k = divmod(n, KF // 4)
                load(R_DOWN + n // 4, n % 4, rows(w_down, 4 * k, 4, 512 * g, 512))
            for t in range(TT):
                sp.wait_ge(resid_ready, TT + t + 1)
                sp.dma_start(out[0, t * P:(t + 1) * P, :], resid[:, t, :]).then_inc(stored, 16)
            sp.wait_ge(stored, 16 * TT)

        @block.gpsimd
        def _(pool):
            pool.memset(wg[:], 0.0).then_inc(zeroed, 1)
            pool.memset(ident[:], 0.0).then_inc(zeroed, 1)
            pool.memset(sel[:], 0.0).then_inc(zeroed, 1)
            pool.memset(causal[:], 0.0).then_inc(zeroed, 1)
            pool.iota(rel[:, 0:2 * P], [[1, 2 * P]], base=0, channel_multiplier=-1,
                      allow_small_or_imprecise_dtypes=True).then_inc(zeroed, 1)
            pool.iota(rel[:, 2 * P:3 * P], [[1, P]], base=0, channel_multiplier=-1,
                      allow_small_or_imprecise_dtypes=True).then_inc(zeroed, 1)
            pool.wait_ge(zeroed, 6)
            pool.affine_select(ident[:], ident[:], [[-1, P]], ALU.not_equal, 1.0, base=0,
                               channel_multiplier=1).then_inc(consts, 1)
            pool.affine_select(sel[:], sel[:], [[-1, HEADS], [0, P]], ALU.not_equal, 1.0, base=0,
                               channel_multiplier=1).then_inc(consts, 1)
            pool.affine_select(causal[:], causal[:], [[0, 2], [1, P]], ALU.is_ge, -1e30, base=0,
                               channel_multiplier=-1).then_inc(consts, 1)
            for c in (0, 2):
                pool.affine_select(rel[:, c * P:(c + 1) * P], rel[:, c * P:(c + 1) * P], [[1, P]],
                                   ALU.is_ge, 1e9, base=0, channel_multiplier=-1).then_inc(consts, 1)
            pool.memset(pre[:, :, 0:CONV - 1], 0.0).then_inc(consts, 1)
            pool.memset(v_sb[:, :, 0:HEADS, HD:HD + 1], 1.0).then_inc(consts, 1)
            pool.memset(v_sb[:, :, HEADS:2 * HEADS, HD:HD + 1], 0.0).then_inc(consts, 1)
            pool.memset(floor[:, :, HEADS:2 * HEADS], 1.0).then_inc(consts, 1)
            pool.dma_start(wg[:, :, 0:HEADS], w_in[:, 4 * DH:4 * DH + HEADS].rearrange(
                "(k p) c -> p k c", p=P)).then_inc(wg_in, 16)
            pool.dma_start(wg[:, :, 32:32 + HEADS], w_in[:, 4 * DH + HEADS:COL_RET].rearrange(
                "(k p) c -> p k c", p=P)).then_inc(wg_in, 16)
            pool.wait_ge(probs_ready, 2 * HEADS)
            pool.dma_start(g_post1[:], g_mix_post[0:1, :].partition_broadcast(P)).then_inc(post_in, 16)
            pool.wait_ge(sub_done, 8 * R_DOWN)
            pool.dma_start(g_post2[:], g_ffn_post[0:1, :].partition_broadcast(P)).then_inc(post_in, 16)

        @block.scalar
        def _(act):
            for src, r0, n in ((g_mix_pre, C_GPRE, 16), (g_ffn_pre, C_GFFN, 16),
                               (conv_b, C_CONVB, 16), (g_mlstm_head, C_GHEAD, 8),
                               (g_ret_head, C_GHEAD + 8, 8)):
                act.dma_start(right[r0:r0 + n, 0, 0:P], src[0, :].rearrange("(r c) -> r c", c=P))\
                   .then_inc(small_in, 16)
            act.dma_start(right[C_CONVW:C_CONVW + 64, 0, 0:P],
                          conv_w[0].rearrange("j (r c) -> (j r) c", c=P)).then_inc(small_in, 16)
            act.dma_start(vec[0:HEADS, 2:3], b_igate[0, :].rearrange("(h o) -> h o", o=1)).then_inc(small_in, 16)
            act.dma_start(vec[32:32 + HEADS, 2:3], b_fgate[0, :].rearrange("(h o) -> h o", o=1)).then_inc(small_in, 16)
            act.dma_start(vec[:, 0:1], inv_freq).then_inc(small_in, 16)
            act.dma_start(cosT[:].bitcast(I32), positions[0:1, :].partition_broadcast(P)).then_inc(small_in, 16)

            def hi(rnd, s):
                rnd, s = rnd + s // 8, s % 8
                act.wait_ge(raw_full[s // 2], 16 * (rnd + 1))
                act.activation(w_hi[:, s % AHEAD, :], raw[:, s // 2, (s % 2) * SUB:(s % 2 + 1) * SUB],
                               ACT.Copy).then_inc(hi_done, 1)

            def ahead(rnd, s):
                act.wait_ge(sub_done, 8 * rnd + s + 1)
                hi(rnd, s + AHEAD)

            def row_norms(var0, junk, resid_there):
                for t in range(TT):
                    resid_there(t)
                    act.activation(junk[:, t, :], resid[:, t, :], ACT.Square,
                                   accum_out=stat[:, S_SQ + t:S_SQ + t + 1]).then_inc(sq_done, 1)
                for t in range(TT):
                    act.wait_ge(var_ready, var0 + t + 1)
                    act.activation(stat[:, S_SD + t:S_SD + t + 1], stat[:, S_VAR + t:S_VAR + t + 1],
                                   ACT.Sqrt).then_inc(sd_ready, 1)

            def transposed_hi(dst, gain, banks0):
                for k in range(KT):
                    act.wait_ge(xT_done, banks0 + k // 2 + 1)
                    act.activation(dst[:, k, 0:SEQ], bank[:, k // 2, (k % 2) * SEQ:(k % 2 + 1) * SEQ],
                                   ACT.Copy, scale=coef[:, gain + k:gain + k + 1]).then_inc(xT_hi, 1)

            row_norms(0, h0, lambda t: act.wait_ge(x_in[t], 16))
            hi(0, 0)
            hi(0, 1)
            act.wait_ge(coef_ready, 1)
            transposed_hi(hT, C_GPRE, 0)
            hi(0, 2)
            hi(0, 3)
            act.wait_ge(wg_in, 32)
            act.activation(wg_hi[:], wg[:], ACT.Copy).then_inc(wg_rounded, 1)

            act.wait_ge(gates_full, 1)
            act.activation(row(R_RIGHT)[0:40], bank[0:40, 5, SEQ:2 * SEQ], ACT.Copy)\
               .then_inc(gates_act, 1)
            act.wait_ge(gates_dve, 3)
            act.activation(row(R_EXP)[32:40], row(R_ABS)[32:40], ACT.Exp, scale=-1.0)\
               .then_inc(gates_act, 1)
            act.wait_ge(gates_act, 2)
            act.activation(row(R_LN)[32:40], row(R_EXP)[32:40], ACT.Ln, bias=1.0)\
               .then_inc(gates_act, 1)
            act.wait_ge(gates_dve, 10)
            act.activation(row(R_FLOOR)[0:HEADS], row(R_NEGROW)[0:HEADS], ACT.Exp)\
               .then_inc(gates_act, 1)
            act.wait_ge(consts, CONSTS)
            for h in range(HEADS):
                act.activation(decay[:, HEADS + h, :], rel[:], ACT.Exp, scale=LOG_GAMMA[h])\
                   .then_inc(decay_ready, 1)

            with act.Fori(0, 4) as r:
                for s in range(8):
                    ahead(r, s)

            def mlstm_decay(h):
                act.wait_ge(masked, h + 1)
                m, o = row(R_MASKED + h % 2), row(R_OPEN + h % 2)
                act.activation(decay[:, h, 0:P], m[:, 0:P], ACT.Exp, bias=a_col[:, 0, h:h + 1])
                act.activation(decay[:, h, P:2 * P], o[:, 0:P], ACT.Exp, bias=a_col[:, 0, h:h + 1])
                act.activation(decay[:, h, 2 * P:3 * P], m[:, P:2 * P], ACT.Exp,
                               bias=a_col[:, 1, h:h + 1]).then_inc(decay_ready, 1)

            def copy_right(pair, event):
                act.wait_ge(acc_free, event + 2)
                act.activation(right[:], acc(pair)[:, :, SEQ:2 * SEQ], ACT.Copy)\
                   .then_inc(right_ready, 1)

            def unit_done(rnd, s):
                group, part = divmod(rnd - R_IN, 3)
                event, two = event_of(rnd, s // 4), slice(2 * (s // 4), 2 * (s // 4) + 2)
                copy_right(s // 4, event)
                if part == 2:
                    act.wait_ge(acc_free, event + 3)
                    act.activation(sg if group >= 2 else gT[:, two, :], gT[:, two, :], ACT.Sigmoid)\
                       .then_inc(sig_done, 1)
                elif group < 2:
                    act.wait_ge(conv_done, sum(e < event for e in with_conv) + 1)
                    act.activation(sg, (qT, kT)[part][:, two, :], ACT.Sigmoid).then_inc(sig_done, 1)

            with_conv = [event_of(r, u) for r in range(R_IN, gate_round(1)) for u in range(2)
                         if (r - R_IN) % 3 < 2]

            def head_norm(a):
                act.wait_ge(pv_done, a + 1)
                act.activation(stat[:, S_DEN:S_DEN + 2], pv_out(a)[:, :, HD], ACT.Abs).then_inc(den_ready, 1)
                act.wait_ge(recip_ready, a + 1)
                for t in range(TT):
                    if t:
                        act.wait_ge(sq_done, Q_HEADS + TT * a + t)
                    act.activation(bank[:, B_PV + a % 2, 384:512], pv_out(a)[:, t, 0:HD], ACT.Square,
                                   scale=stat[:, S_RECIP + t:S_RECIP + t + 1],
                                   accum_out=stat[:, S_HSQ + t:S_HSQ + t + 1]).then_inc(sq_done, 1)
                act.wait_ge(var_ready, V_HEADS + a + 1)
                act.activation(stat[:, S_HSD:S_HSD + 2], stat[:, S_HVAR:S_HVAR + 2], ACT.Sqrt)\
                   .then_inc(sd_ready, 1)

            def mix_round(a):
                act.wait_ge(mix_ready, a + 1)
                act.activation(mixT[:, a, 0:SEQ], gT[:, a % 4, :], ACT.Copy).then_inc(mix_hi, 1)

            def attention_steps(rnd, s):
                a = head_at(rnd, s, 4)
                if a is not None:
                    mix_round(a)
                a = head_at(rnd, s, 1)
                if a is not None:
                    head_norm(a)

            for rnd in range(R_IN, R_OUT):
                for s in range(8):
                    ahead(rnd, s)
                    if rnd == R_IN:
                        mlstm_decay(s)
                    if s % 4 == 3:
                        unit_done(rnd, s)
                    if rnd == R_IN + 1 and s == 4:
                        act.wait_ge(angles, 1)
                        act.activation(sinT[:], row(2), ACT.Sin, scale=vec[:, 1:2]).then_inc(rope_ready, 1)
                        act.wait_ge(angles, 2)
                        act.activation(cosT[:], row(3), ACT.Sin).then_inc(rope_ready, 1)
                    attention_steps(rnd, s)

            def squares(pair, subs, g, count):
                act.wait_ge(sub_done, subs)
                for t in range(TT):
                    act.wait_ge(sq_done, count + TT * g + t)
                    act.activation(bank[:, B_S, :], acc(pair)[:, t, :], ACT.Square,
                                   accum_out=stat[:, S_PSQ + 4 * t + g:S_PSQ + 4 * t + g + 1])\
                       .then_inc(sq_done, 1)

            for rnd in range(R_OUT, R_FF):
                for s in range(8):
                    ahead(rnd, s)
                    attention_steps(rnd, s)
                squares(rnd % 2, 8 * rnd + 8, rnd - R_OUT, Q_POST1)

            def post_root(count):
                act.wait_ge(var_ready, count)
                act.activation(stat[:, S_PSD:S_PSD + 2], stat[:, S_PVAR:S_PVAR + 2], ACT.Sqrt)\
                   .then_inc(sd_ready, 1)

            post_root(V_POST1)
            row_norms(V_NORM2, mixed, lambda t: act.wait_ge(resid_ready, t + 1))
            transposed_hi(h2T, C_GFFN, KT // 2)

            with act.Fori(0, PAIRS) as i:
                for s in range(8):
                    ahead(i + R_FF, s)
                    if s == 3:
                        copy_right(0, 2 * i + E_FF)
                    if s == 4:
                        act.wait_ge(acc_free, 2 * i + (E_FF + 3))
                        act.activation(ff_g[:], ff_g[:], ACT.Silu).then_inc(silu_done, 1)
                    if s == 7:
                        copy_right(1, 2 * i + (E_FF + 1))
                        act.wait_ge(ff_ready, i + 1)
                        act.activation(ffT[:, bass.ds(2 * i, 2), 0:SEQ], ff_u[:], ACT.Copy)\
                           .then_inc(ff_hi, 1)

            for n in range(4 * DOWN_SUBS):
                if 8 * R_DOWN + n + AHEAD < N_SUBS:
                    ahead(R_DOWN, n)
                g, s = divmod(n, DOWN_SUBS)
                if s == DOWN_SUBS - 1:
                    squares(g % 2, 8 * R_DOWN + n + 1, g, Q_POST2)
            post_root(V_POST2)

        @block.vector
        def _(dve):
            steps = [0]

            def link(ins):
                steps[0] += 1
                ins.then_inc(dve_step, 1)
                dve.wait_ge(dve_step, steps[0])

            def lo(rnd, s):
                rnd, s = rnd + s // 8, s % 8
                dve.wait_ge(hi_done, 8 * rnd + s + 1)
                dve.tensor_tensor(w_lo[:, s % AHEAD, :], raw[:, s // 2, (s % 2) * SUB:(s % 2 + 1) * SUB],
                                  w_hi[:, s % AHEAD, :].bitcast(F32), ALU.subtract).then_inc(lo_done, 1)

            def row_norms(dst, sq0, sd0):
                for t in range(TT):
                    dve.wait_ge(sq_done, sq0 + t + 1)
                    dve.tensor_scalar(stat[:, S_VAR + t:S_VAR + t + 1], stat[:, S_SQ + t:S_SQ + t + 1],
                                      1.0 / D, EPS, ALU.mult, ALU.add).then_inc(var_ready, 1)
                for t in range(TT):
                    dve.wait_ge(sd_ready, sd0 + t + 1)
                    link(dve.reciprocal(stat[:, S_RSTD + t:S_RSTD + t + 1], stat[:, S_SD + t:S_SD + t + 1]))
                    dve.tensor_scalar(dst[:, t, :], resid[:, t, :], stat[:, S_RSTD + t:S_RSTD + t + 1],
                                      None, ALU.mult).then_inc(h_ready, 1)

            def transposed_lo(dst, gain, tiles0):
                for k in range(KT):
                    dve.wait_ge(xT_hi, tiles0 + 2 * (k // 2) + 2)
                    dve.scalar_tensor_tensor(
                        dst[:, k, SEQ:2 * SEQ], bank[:, k // 2, (k % 2) * SEQ:(k % 2 + 1) * SEQ],
                        coef[:, gain + k:gain + k + 1], dst[:, k, 0:SEQ].bitcast(F32),
                        ALU.mult, ALU.subtract).then_inc(xT_lo, 1)

            dve.memset(vec[0:64, 1:2], 1.0)
            dve.memset(vec[64:128, 1:2], -1.0)
            dve.memset(stat[:, 62:63], 0.0).then_inc(acc_free, 2)
            dve.memset(stat[:, 63:64], 0.0).then_inc(y_ready, 2)
            dve.wait_ge(coef_T, 1)
            dve.tensor_copy(coef[:], bank[:, 7, 0:P]).then_inc(coef_ready, 1)
            row_norms(h0, 0, 0)
            lo(0, 0)
            lo(0, 1)
            dve.wait_ge(coef_ready, 1)
            transposed_lo(hT, C_GPRE, 0)
            lo(0, 2)
            lo(0, 3)
            dve.wait_ge(wg_rounded, 1)
            dve.tensor_tensor(wg_lo[:], wg[:], wg_hi[:].bitcast(F32), ALU.subtract).then_inc(wg_ready, 1)

            def gates(ins, n):
                ins.then_inc(gates_dve, 1)
                dve.wait_ge(gates_dve, n)

            def rowi(n):
                return row(n)[0:HEADS]

            def rowf(n):
                return row(n)[32:32 + HEADS]

            dve.wait_ge(gates_act, 1)
            for n, p0 in enumerate((0, 32)):
                gates(dve.scalar_tensor_tensor(row(R_Z)[p0:p0 + HEADS], bank[p0:p0 + HEADS, 5, 0:SEQ],
                                               vec[p0:p0 + HEADS, 2:3], row(R_RIGHT)[p0:p0 + HEADS],
                                               ALU.add, ALU.add), n + 1)
            gates(dve.scalar_tensor_tensor(rowf(R_ABS), rowf(R_Z), -1.0, rowf(R_Z), ALU.mult, ALU.max), 3)
            link(dve.memset(rowf(R_ONES), 1.0))
            dve.wait_ge(gates_act, 3)
            gates(dve.scalar_tensor_tensor(rowf(R_A), rowf(R_Z), 0.0, rowf(R_LN), ALU.min, ALU.subtract), 4)
            gates(dve.tensor_tensor_scan(rowf(R_F), rowf(R_ONES), rowf(R_A), 0.0, ALU.mult, ALU.add), 5)
            gates(dve.tensor_copy(rowi(R_F), rowf(R_F)), 6)
            gates(dve.tensor_tensor(rowi(R_A), rowi(R_Z), rowi(R_F), ALU.subtract), 7)
            gates(dve.tensor_tensor_scan(rowi(R_M), rowi(R_A), rowi(R_A), 0.0, ALU.max, ALU.max), 8)
            gates(dve.tensor_scalar(rowi(R_NEGM), rowi(R_M), -1.0, None, ALU.mult), 9)
            gates(dve.scalar_tensor_tensor(rowi(R_NEGROW), rowi(R_F), -1.0, rowi(R_M), ALU.mult,
                                           ALU.subtract), 10)

            with dve.Fori(0, 2) as i:
                for e in range(2):
                    for s in range(8):
                        lo(2 * i + e, s + AHEAD)
                    dve.wait_ge(sub_done, 16 * i + (8 * e + 8))
                    for t in range(TT):
                        ins = dve.tensor_copy(v_sb[:, t, bass.ds(8 * i + 4 * e, 4), 0:HD],
                                              acc(e)[:, t, :].rearrange("p (h c) -> p h c", c=HD))
                    ins.then_inc(acc_free, 1)

            dve.wait_ge(cols_T, 1)
            cols = bank[:, 4, 0:4 * HEADS].rearrange("p (n t h) -> p n t h", n=2, t=TT)
            dve.tensor_copy(a_col[:], cols[:, 0])
            dve.wait_ge(consts, CONSTS)
            dve.tensor_copy(floor[:, :, 0:HEADS], cols[:, 1]).then_inc(cols_ready, 1)

            def mask_exponents(h):
                dve.wait_ge(spread_done, h + 1)
                if h >= 2:
                    dve.wait_ge(decay_ready, HEADS + h - 1)
                dve.tensor_tensor(row(R_MASKED + h % 2), spread(h),
                                  causal[:].rearrange("p t c -> p (t c)"), ALU.add)
                dve.tensor_copy(row(R_OPEN + h % 2)[:, 0:P], spread(h)[:, P:2 * P]).then_inc(masked, 1)

            def rope_angles():
                pos, ang, turns = row(0), row(1), row(4)
                dve.wait_ge(small_in, SMALL)
                link(dve.tensor_copy(pos, cosT[:].bitcast(I32)))
                link(dve.tensor_scalar(ang, pos, vec[:, 0:1], None, ALU.mult))
                for dst, quarter in ((row(2), 0.0), (row(3), 0.25)):
                    link(dve.tensor_scalar(turns, ang, 1.0 / (2 * math.pi), quarter, ALU.mult, ALU.add))
                    link(dve.tensor_scalar(turns, turns, ROUND, None, ALU.add))
                    link(dve.tensor_scalar(turns, turns, ROUND, quarter, ALU.subtract, ALU.subtract))
                    link(dve.scalar_tensor_tensor(dst, turns, -TWO_PI_1, ang, ALU.mult, ALU.add))
                    link(dve.scalar_tensor_tensor(dst, turns, -TWO_PI_2, dst, ALU.mult, ALU.add))
                    link(dve.scalar_tensor_tensor(dst, turns, -TWO_PI_3, dst, ALU.mult, ALU.add))
                    dve.tensor_scalar(dst, dst, -3.1415925, 3.1415925, ALU.max, ALU.min).then_inc(angles, 1)

            def unit_done(rnd, s):
                group, part = divmod(rnd - R_IN, 3)
                u = s // 4
                event, two = event_of(rnd, u), slice(2 * u, 2 * u + 2)
                dst = (qT, kT, gT)[part]
                dve.wait_ge(right_ready, event - E_IN + 1)
                summed = gT[:, two, :] if part == 2 else pre[:, :, CONV - 1:]
                dve.tensor_tensor(summed, acc(u)[:, :, 0:SEQ], right[:], ALU.add).then_inc(acc_free, 1)
                dve.wait_ge(acc_free, event + 3)
                if part == 2:
                    if group >= 2:
                        dve.wait_ge(sig_done, sig_count(event))
                        link(dve.tensor_tensor(gT[:, two, :], gT[:, two, :], sg, ALU.mult))
                    return
                if group < 2:
                    for j in range(CONV):
                        for c in range(2):
                            tile = HEADS * part + 4 * group + 2 * u + c
                            tap = coef[:, C_CONVW + 16 * j + tile:C_CONVW + 16 * j + tile + 1]
                            src = pre[:, c, j:j + SEQ]
                            if j == 0:
                                ins = dve.tensor_scalar(dst[:, 2 * u + c, :], src, tap,
                                                        coef[:, C_CONVB + tile:C_CONVB + tile + 1],
                                                        ALU.mult, ALU.add)
                            else:
                                ins = dve.scalar_tensor_tensor(dst[:, 2 * u + c, :], src, tap,
                                                               dst[:, 2 * u + c, :], ALU.mult, ALU.add)
                        if j < CONV - 1:
                            link(ins)
                    ins.then_inc(conv_done, 1)
                    dve.wait_ge(sig_done, sig_count(event))
                    ins = dve.tensor_tensor(dst[:, two, :], dst[:, two, :], sg, ALU.mult)
                else:
                    dve.wait_ge(rope_ready, 2)
                    for c in range(2):
                        src = pre[:, c, CONV - 1:]
                        dve.tensor_tensor(spin[0:64, c, :], src[64:128], sinT[64:128, :], ALU.mult)
                        dve.tensor_tensor(spin[64:128, c, :], src[0:64], sinT[0:64, :], ALU.mult)
                        link(dve.tensor_tensor(dst[:, 2 * u + c, :], src, cosT[:], ALU.mult))
                    ins = dve.tensor_tensor(dst[:, two, :], dst[:, two, :], spin, ALU.add)
                if part == 1:
                    ins.then_inc(qk_ready, 2)
                    dve.wait_ge(qk_ready, 4 * group + 2 * u + 2)
                else:
                    link(ins)

            def weigh(a):
                dve.wait_ge(scores_done, a + 1)
                dve.wait_ge(decay_ready, HEADS + min(a + 1, HEADS))
                if a >= 1:
                    dve.wait_ge(pv_done, a)
                dve.scalar_tensor_tensor(probs[:], bank[:, B_S, 0:3 * P], SCALE, decay[:, a, :],
                                         ALU.mult, ALU.mult).then_inc(probs_ready, 1)

            def head_norm(a):
                col = lambda c: stat[:, c:c + 2]
                dve.wait_ge(den_ready, a + 1)
                link(dve.tensor_tensor(col(S_DEN), col(S_DEN), floor[:, :, a], ALU.max))
                dve.reciprocal(col(S_RECIP), col(S_DEN)).then_inc(recip_ready, 1)
                dve.wait_ge(sq_done, Q_HEADS + TT * (a + 1))
                dve.tensor_scalar(col(S_HVAR), col(S_HSQ), 1.0 / HD, EPS, ALU.mult, ALU.add)\
                   .then_inc(var_ready, 1)
                dve.wait_ge(sd_ready, V_HEADS + a + 1)
                link(dve.reciprocal(col(S_HRSTD), col(S_HSD)))
                link(dve.tensor_tensor(col(S_HSCALE), col(S_HRSTD), col(S_RECIP), ALU.mult))
                if a >= 2:
                    dve.wait_ge(yT_done, a - 1)
                for t in range(TT):
                    ins = dve.tensor_scalar(y[:, a % 2, t, :], pv_out(a)[:, t, 0:HD],
                                            stat[:, S_HSCALE + t:S_HSCALE + t + 1], None, ALU.mult)
                ins.then_inc(y_ready, 1)

            def mix(a):
                dve.wait_ge(yT_done, a + 1)
                dve.wait_ge(sig_done, sig_count(event_of(gate_round(a // 4), a % 4 // 2)))
                dve.scalar_tensor_tensor(gT[:, a % 4, :], bank[:, B_T, 0:SEQ],
                                         coef[:, C_GHEAD + a:C_GHEAD + a + 1], gT[:, a % 4, :],
                                         ALU.mult, ALU.mult).then_inc(mix_ready, 1)
                dve.wait_ge(mix_hi, a + 1)
                dve.tensor_tensor(mixT[:, a, SEQ:2 * SEQ], gT[:, a % 4, :],
                                  mixT[:, a, 0:SEQ].bitcast(F32), ALU.subtract).then_inc(mix_lo, 1)

            def attention_steps(rnd, s):
                a = head_at(rnd, s, 4)
                if a is not None:
                    mix(a)
                a = head_at(rnd, s, 1)
                if a is not None:
                    head_norm(a)
                a = head_at(rnd, s, 0)
                if a is not None:
                    weigh(a)

            for rnd in range(R_IN, R_OUT):
                for s in range(8):
                    lo(rnd, s + AHEAD)
                    if rnd == R_IN:
                        mask_exponents(s)
                    if rnd == R_IN + 1 and s == 2:
                        rope_angles()
                    if s % 4 == 3:
                        unit_done(rnd, s)
                    attention_steps(rnd, s)

            def emptied(pair, dst, gain, g, squares_done):
                dve.wait_ge(sq_done, squares_done)
                for t in range(TT):
                    ins = dve.tensor_tensor(dst[:, t, 512 * g:512 * (g + 1)], acc(pair)[:, t, :],
                                            gain[:, 512 * g:512 * (g + 1)], ALU.mult)
                ins.then_inc(acc_free, 1)

            def add_normed(src, acc_count, count, sd_count):
                dve.wait_ge(acc_free, acc_count)
                link(dve.tensor_reduce(stat[:, S_PSUM:S_PSUM + 2],
                                       stat[:, S_PSQ:S_PSQ + 8].rearrange("p (t g) -> p t g", t=TT),
                                       mybir.AxisListType.X, ALU.add))
                dve.tensor_scalar(stat[:, S_PVAR:S_PVAR + 2], stat[:, S_PSUM:S_PSUM + 2],
                                  1.0 / D, EPS, ALU.mult, ALU.add).then_inc(var_ready, 1)
                dve.wait_ge(sd_ready, sd_count)
                link(dve.reciprocal(stat[:, S_PRSTD:S_PRSTD + 2], stat[:, S_PSD:S_PSD + 2]))
                for t in range(TT):
                    dve.scalar_tensor_tensor(resid[:, t, :], src[:, t, :],
                                             stat[:, S_PRSTD + t:S_PRSTD + t + 1], resid[:, t, :],
                                             ALU.mult, ALU.add).then_inc(resid_ready, 1)
                dve.wait_ge(resid_ready, count)

            for rnd in range(R_OUT, R_FF):
                g = rnd - R_OUT
                for s in range(8):
                    lo(rnd, s + AHEAD)
                    attention_steps(rnd, s)
                if g == 0:
                    dve.wait_ge(post_in, 16)
                emptied(rnd % 2, mixed, g_post1, g, Q_POST1 + TT * (g + 1))
            add_normed(mixed, E_FF + 2, TT, V_POST1)
            row_norms(mixed, Q_NORM2, V_NORM2)
            transposed_lo(h2T, C_GFFN, KT)

            with dve.Fori(0, PAIRS) as i:
                for s in range(8):
                    lo(i + R_FF, s + AHEAD)
                    if s == 3:
                        dve.wait_ge(right_ready, 2 * i + (E_OUT - E_IN + 1))
                        dve.tensor_tensor(ff_g[:], acc(0)[:, :, 0:SEQ], right[:], ALU.add).then_inc(acc_free, 1)
                    if s == 7:
                        dve.wait_ge(right_ready, 2 * i + (E_OUT - E_IN + 2))
                        dve.tensor_tensor(ff_u[:], acc(1)[:, :, 0:SEQ], right[:], ALU.add).then_inc(acc_free, 1)
                        dve.wait_ge(acc_free, 2 * i + (E_FF + 4))
                        dve.wait_ge(silu_done, i + 1)
                        dve.tensor_tensor(ff_u[:], ff_u[:], ff_g[:], ALU.mult).then_inc(ff_ready, 1)
                        dve.wait_ge(ff_hi, i + 1)
                        dve.tensor_tensor(ffT[:, bass.ds(2 * i, 2), SEQ:2 * SEQ], ff_u[:],
                                          ffT[:, bass.ds(2 * i, 2), 0:SEQ].bitcast(F32), ALU.subtract)\
                           .then_inc(ff_lo, 1)

            for n in range(4 * DOWN_SUBS):
                if 8 * R_DOWN + n + AHEAD < N_SUBS:
                    lo(R_DOWN, n + AHEAD)
                g, s = divmod(n, DOWN_SUBS)
                if s == DOWN_SUBS - 1:
                    if g == 0:
                        dve.wait_ge(post_in, 32)
                    emptied(g % 2, ff_out, g_post2, g, Q_POST2 + TT * (g + 1))
            add_normed(ff_out, E_DOWN + 4 + 2, 2 * TT, V_POST2)

        @block.tensor
        def _(pe):
            def mm(out_, lhsT, rhs, start, stop):
                return pe.matmul(out_, lhsT, rhs, start=start, stop=stop, skip_group_check=True)

            def transposed(src, done, h_count, before=lambda b: None):
                for t in range(TT):
                    pe.wait_ge(h_ready, h_count + t + 1)
                for b in range(KT // 2):
                    before(b)
                    for k in range(2):
                        for t in range(TT):
                            ins = pe.transpose(bank[:, b, k * SEQ + t * P:k * SEQ + (t + 1) * P],
                                               src[:, t, (2 * b + k) * P:(2 * b + k + 1) * P], ident[:])
                    ins.then_inc(xT_done, 1)

            def sub_columns(rnd, s, act_T, pair):
                pe.wait_ge(lo_done, 8 * rnd + s + 1)
                slot, quarter = s % AHEAD, s % 4
                for c in range(2):
                    for j in range(4):
                        k = 4 * quarter + j
                        cols = slice(256 * j + P * c, 256 * j + P * (c + 1))
                        mm(bank[:, 2 * pair + c, :], w_hi[:, slot, cols], act_T[:, k, :], k == 0, False)
                        ins = mm(bank[:, 2 * pair + c, 0:SEQ], w_lo[:, slot, cols], act_T[:, k, 0:SEQ],
                                 False, k == KT - 1)
                ins.then_inc(sub_done, 1)

            def unit_columns(rnd, unit, event, act_T, before=None, after=None):
                pe.wait_ge(acc_free, event + 1)
                for q in range(4):
                    s = 4 * unit + q
                    if before:
                        before(s)
                    sub_columns(rnd, s, act_T, unit)
                    if after:
                        after(s)

            def sub_tokens(count, slot, act_T, pair, k0, last):
                pe.wait_ge(lo_done, count)
                for j in range(2):
                    k, w = k0 + j, slice(512 * j, 512 * (j + 1))
                    for t in range(TT):
                        hi_x = act_T[:, k, t * P:(t + 1) * P]
                        lo_x = act_T[:, k, SEQ + t * P:SEQ + (t + 1) * P]
                        mm(bank[:, 2 * pair + t, :], hi_x, w_hi[:, slot, w], k == 0, False)
                        mm(bank[:, 2 * pair + t, :], hi_x, w_lo[:, slot, w], False, False)
                        ins = mm(bank[:, 2 * pair + t, :], lo_x, w_hi[:, slot, w], False, k == last)
                ins.then_inc(sub_done, 1)

            pe.wait_ge(consts, 1)
            pe.wait_ge(small_in, SMALL)
            pe.transpose(bank[:, 7, 0:P], right[:, 0, 0:P], ident[:]).then_inc(coef_T, 1)
            transposed(h0, 0, 0, lambda b: pe.wait_ge(coef_ready, 1) if b == 7 else None)

            pe.wait_ge(wg_ready, 1)
            pe.wait_ge(xT_lo, KT)
            for k in range(KT):
                mm(bank[0:40, 5, :], wg_hi[:, k, :], hT[:, k, :], k == 0, False)
                ins = mm(bank[0:40, 5, 0:SEQ], wg_lo[:, k, :], hT[:, k, 0:SEQ], False, k == KT - 1)
            ins.then_inc(gates_full, 1)

            with pe.Fori(0, 2) as i:
                for e in range(2):
                    pe.wait_ge(acc_free, 2 * i + (e + 1))
                    for s in range(8):
                        sub_tokens(16 * i + (8 * e + s + 1), s % AHEAD, hT, e, 2 * s, KT - 1)

            pe.wait_ge(gates_act, 4)
            pe.wait_ge(gates_dve, 10)
            for n, r in enumerate((R_A, R_FLOOR)):
                for t in range(TT):
                    c = (TT * n + t) * HEADS
                    ins = pe.transpose(bank[:, 4, c:c + HEADS], row(r)[0:HEADS, t * P:(t + 1) * P],
                                       ident[0:HEADS, 0:HEADS])
            ins.then_inc(cols_T, 1)
            pe.wait_ge(consts, CONSTS)
            pe.wait_ge(cols_ready, 1)
            for h in range(HEADS):
                mm(spread(h), sel[:, h, :], row(R_NEGM)[0:HEADS], True, True).then_inc(spread_done, 1)

            def scores(group, n):
                pe.wait_ge(qk_ready, 4 * group + (n + 1))
                mm(bank[:, B_S, 0:SEQ], kT[:, n, 0:P], qT[:, n, :], True, True)
                mm(bank[:, B_S, SEQ:SEQ + P], kT[:, n, P:2 * P], qT[:, n, P:2 * P], True, True)\
                    .then_inc(scores_done, 1)

            def weighted(group, n):
                pe.wait_ge(probs_ready, 4 * group + (n + 1))
                pe.wait_ge(y_ready, 4 * group + (n + 1))
                o = bank[:, B_PV + n % 2, :]
                v = v_sb[:, :, bass.ds(4 * group + n, 1), :].rearrange("p t o c -> p t (o c)")
                mm(o[:, 0:HD + 1], probs[:, 0:P], v[:, 0, :], True, True)
                mm(o[:, HD + 1:2 * (HD + 1)], probs[:, P:2 * P], v[:, 0, :], False, False)
                mm(o[:, HD + 1:2 * (HD + 1)], probs[:, 2 * P:3 * P], v[:, 1, :], False, True)\
                    .then_inc(pv_done, 1)

            def turned(group, n):
                pe.wait_ge(y_ready, 4 * group + (n + 3))
                if n:
                    pe.wait_ge(mix_ready, 4 * group + n)
                for t in range(TT):
                    ins = pe.transpose(bank[:, B_T, t * P:(t + 1) * P], y[:, n % 2, t, :], ident[:])
                ins.then_inc(yT_done, 1)

            def gate_units(group, rnd, event):
                def before(s):
                    if s % 2 == 0:
                        scores(group, s // 2)

                def after(s):
                    if s % 2 == 1:
                        weighted(group, s // 2)
                    if s >= 4 and s % 2 == 0:
                        turned(group, (s - 4) // 2)

                for u in range(2):
                    unit_columns(rnd, u, event + u, hT, before, after)

            def left_over(group):
                return lambda s: turned(group, 2 + s // 2) if s in (0, 2) else None

            for n in range(2):
                for u in range(2):
                    unit_columns(R_IN + n, u, event_of(R_IN + n, u), hT)
            with pe.Fori(0, 3) as j:
                gate_units(j, 3 * j + gate_round(0), 6 * j + event_of(gate_round(0), 0))
                for n in (1, 2):
                    for u in range(2):
                        unit_columns(3 * j + (gate_round(0) + n), u,
                                     6 * j + event_of(gate_round(0) + n, u), hT,
                                     after=left_over(j) if n == 1 else None)
            gate_units(3, gate_round(3), event_of(gate_round(3), 0))

            for g in range(4):
                pe.wait_ge(acc_free, E_OUT + g + 1)
                for s in range(8):
                    if g == 0:
                        pe.wait_ge(mix_lo, 2 * s + 2)
                    sub_tokens(8 * (R_OUT + g) + s + 1, s % AHEAD, mixT, g % 2, 2 * s, KT - 1)
                    if g == 0:
                        left_over(3)(s)

            transposed(mixed, KT // 2, TT)
            pe.wait_ge(xT_lo, 2 * KT)
            with pe.Fori(0, PAIRS) as i:
                for u in range(2):
                    unit_columns(i + R_FF, u, 2 * i + (E_FF + u), h2T)

            for g in range(4):
                pe.wait_ge(acc_free, E_DOWN + g + 1)
                for s in range(DOWN_SUBS):
                    n = DOWN_SUBS * g + s
                    if g == 0:
                        pe.wait_ge(ff_lo, s + 1)
                    sub_tokens(8 * R_DOWN + n + 1, n % AHEAD, ffT, g % 2, 2 * s, KF - 1)


_INS = ["x", "positions", "g_mix_pre", "w_in", "conv_w", "conv_b", "b_igate", "b_fgate",
        "g_mlstm_head", "g_ret_head", "w_out", "g_mix_post", "g_ffn_pre", "w_gate", "w_up", "w_down",
        "g_ffn_post"]


def kernel(**inputs):
    import concourse.bacc as bacc
    from concourse.bass_utils import run_bass_kernel_spmd

    nc = bacc.Bacc("TRN2", target_bir_lowering=False, num_devices=1)
    arrays, args = {}, []
    steps = np.arange(0, HD, 2, dtype=np.float32) / np.float32(HD)
    inv_freq = np.power(np.float32(10000.0), -steps).astype(np.float32)
    constants = {"inv_freq": np.concatenate([inv_freq, inv_freq]).reshape(P, 1)}
    for name in _INS + ["inv_freq"]:
        a = np.ascontiguousarray(constants[name] if name in constants else inputs[name])
        if a.ndim == 3 and a.shape[0] == 1 and name.startswith("w_"):
            a = a[0]
        arrays[f"in_{name}"] = a
        args.append(nc.dram_tensor(f"in_{name}", a.shape, mybir.dt.from_np(a.dtype),
                                   kind="ExternalInput").ap())
    out = nc.dram_tensor("out_0", (1, SEQ, D), F32, kind="ExternalOutput").ap()
    hybrid_layer(nc, *args, out)
    r = run_bass_kernel_spmd(nc, [arrays], core_ids=[0])
    return r.results[0]["out_0"]
```

```python
import math
from contextlib import ExitStack

import numpy as np

import concourse.bass as bass
from concourse import mybir

ALU = mybir.AluOpType
ACT = mybir.ActivationFunctionType
F32 = mybir.dt.float32
F32R = mybir.dt.float32r
I32 = mybir.dt.int32

P = 128
SEQ = 256
D = 2048
HD = 128
HEADS = 8
DH = HEADS * HD
D_FF = 5632
KT = D // P
KF = D_FF // P
TT = SEQ // P
CONV = 4
EPS = 1e-6
SCALE = HD ** -0.5
COL_RET = 4 * DH + 2 * HEADS

SUB = 1024
RAW_CHUNKS = 4
AHEAD = 4
R_V = 0
R_IN = R_V + 4
R_OUT = R_IN + 12
R_FF = R_OUT + 4
PAIRS = D_FF // 256
R_DOWN = R_FF + PAIRS
DOWN_SUBS = KF // 2
N_SUBS = 8 * R_DOWN + 4 * DOWN_SUBS
E_IN = 4
E_OUT = E_IN + 24
E_FF = E_OUT + 4
E_DOWN = E_FF + 2 * PAIRS
C_GPRE, C_GFFN, C_CONVB, C_GHEAD, C_CONVW = 0, 16, 32, 48, 64

TWO_PI_1 = 6.28125
TWO_PI_2 = float(np.float32(np.float64(2 * np.pi - 6.28125).astype(np.float16)))
TWO_PI_3 = float(np.float32(2 * np.pi - 6.28125 - TWO_PI_2))
ROUND = 1.5 * 2.0 ** 23
LOG_GAMMA = [math.log(1.0 - 2.0 ** (-5.0 - h)) for h in range(HEADS)]


S_SQ, S_VAR, S_SD, S_RSTD = 0, 2, 4, 6
S_PSQ, S_PSUM, S_PVAR, S_PSD, S_PRSTD = 8, 16, 18, 20, 22
S_SPARE = 24
S_HEAD, S_HEAD_COLS = 32, 16
H_DEN, H_RECIP, H_SQ, H_VAR, H_SD, H_RSTD, H_SCALE = range(0, 14, 2)


def event_of(rnd, unit):
    return 2 * rnd - 4 + unit


def gate_round(group):
    return R_IN + 3 * group + 2


def head_at(rnd, s, first):
    for group in range(4):
        n, odd = divmod(8 * (rnd - gate_round(group)) + s - first, 2)
        if not odd and 0 <= n < 4:
            return 4 * group + n
    return None


def unit_at(rnd, s, lag):
    rnd, s = rnd - (lag > s), (s - lag) % 8
    if R_IN <= rnd < R_OUT and s % 4 == 3:
        return (*divmod(rnd - R_IN, 3), s // 4)
    return None


def hybrid_layer(nc, x, positions, g_mix_pre, w_in, conv_w, conv_b, b_igate, b_fgate, g_mlstm_head,
                 g_ret_head, w_out, g_mix_post, g_ffn_pre, w_gate, w_up, w_down, g_ffn_post,
                 inv_freq, out):
    with ExitStack() as ctx:
        def sb(name, shape, dt=F32, stack=ctx):
            return stack.enter_context(nc.sbuf_tensor(name, shape, dt))

        def sem(name):
            return ctx.enter_context(nc.semaphore(name))

        raw = sb("raw", [P, RAW_CHUNKS, 2 * SUB])
        w_hi = sb("w_hi", [P, AHEAD, SUB], F32R)
        w_lo = sb("w_lo", [P, AHEAD, SUB], F32R)
        resid = sb("resid", [P, TT, D])
        columns = sb("columns", [P, 2, P])
        ident, coef = columns[:, 0, :], columns[:, 1, :]
        rms_row = columns[:].rearrange("p a c -> p (a c)")
        right = sb("right", [P, 2, SEQ])
        stat = sb("stat", [P, S_HEAD + 2 * S_HEAD_COLS])

        mixer = ExitStack()
        late = ExitStack()
        mixed = sb("mixed", [P, TT, D], stack=late)
        g_post1 = sb("g_post1", [P, D], stack=late)
        late.close()
        decay = sb("decay", [P, 2 * HEADS, 3 * P], stack=mixer)
        v_sb = sb("v_sb", [P, TT, 2 * HEADS, HD + 1], stack=mixer)
        hT = sb("hT", [P, KT, 2 * SEQ], F32R, stack=mixer)
        start = ExitStack()
        h0 = sb("h0", [P, TT, D], stack=start)
        sel = sb("sel", [HEADS, HEADS, P], stack=start)
        rel = sb("rel", [P, 3 * P], stack=start)
        wg = sb("wg", [P, KT, 40], stack=start)
        wg_hi = sb("wg_hi", [P, KT, 40], F32R, stack=start)
        wg_lo = sb("wg_lo", [P, KT, 40], F32R, stack=start)
        start.close()
        mixT = sb("mixT", [P, KT, 2 * SEQ], F32R, stack=mixer)
        qT = sb("qT", [P, 4, SEQ], stack=mixer)
        kT = sb("kT", [P, 4, SEQ], stack=mixer)
        gT = sb("gT", [P, 4, SEQ], stack=mixer)
        probs = sb("probs", [P, 3 * P], stack=mixer)
        y = sb("y", [P, 2, TT, HD], stack=mixer)
        pre = sb("pre", [P, 2, SEQ + CONV - 1], stack=mixer)
        cosT = sb("cosT", [P, SEQ], stack=mixer)
        sinT = sb("sinT", [P, SEQ], stack=mixer)
        a_col = sb("a_col", [P, TT, HEADS], stack=mixer)
        floor = sb("floor", [P, TT, 2 * HEADS], stack=mixer)
        vec = sb("vec", [P, 4], stack=mixer)
        mixer.close()
        new = pre[:, :, CONV - 1:]
        spin = gT[:, 0:2, :]
        ffn = ExitStack()
        ffT = sb("ffT", [P, KF, 2 * SEQ], F32R, stack=ffn)
        last = ExitStack()
        ff_out = sb("ff_out", [P, TT, D], stack=last)
        g_post2 = sb("g_post2", [P, D], stack=last)
        last.close()
        h2T = sb("h2T", [P, KT, 2 * SEQ], F32R, stack=ffn)
        ff_g = sb("ff_g", [P, 2, SEQ], stack=ffn)
        ff_u = sb("ff_u", [P, 2, SEQ], stack=ffn)
        ctx.callback(ffn.close)

        def row(n):
            return h0[:, n // 8, (n % 8) * SEQ:(n % 8 + 1) * SEQ]

        R_RIGHT, R_Z, R_ABS, R_EXP, R_LN, R_A, R_F, R_M, R_FLOOR, R_NEGM, R_NEGROW, R_ONES = range(12)

        bank = ctx.enter_context(nc.psum_tensor("bank", [P, 8, 512], F32))
        B_S, B_PV, B_T = 4, 5, 7

        def acc(pair):
            return bank[:, 2 * pair:2 * pair + 2, :]

        def spread(h):
            return bank[:, 4 + h // 2, (h % 2) * SEQ:(h % 2 + 1) * SEQ]

        def pv_out(a):
            return bank[:, B_PV + a % 2, 0:TT * (HD + 1)].rearrange("p (t c) -> p t c", t=TT)

        raw_full = [sem(f"raw_full{n}") for n in range(RAW_CHUNKS)]
        hi_done = sem("hi_done")
        lo_done = sem("lo_done")
        sub_done = sem("sub_done")
        acc_free = sem("acc_free")
        right_ready = sem("right_ready")
        x_in = [sem(f"x_in{t}") for t in range(TT)]
        small_in = sem("small_in")
        wg_in = sem("wg_in")
        post_in = sem("post_in")
        zeroed = sem("zeroed")
        consts = sem("consts")
        dve_step = sem("dve_step")
        sq_done = sem("sq_done")
        var_ready = sem("var_ready")
        sd_ready = sem("sd_ready")
        resid_ready = sem("resid_ready")
        h_ready = sem("h_ready")
        xT_done = sem("xT_done")
        xT_hi = sem("xT_hi")
        xT_lo = sem("xT_lo")
        coef_T = sem("coef_T")
        coef_ready = sem("coef_ready")
        wg_rounded = sem("wg_rounded")
        wg_ready = sem("wg_ready")
        gates_full = sem("gates_full")
        gates_act = sem("gates_act")
        gates_dve = sem("gates_dve")
        cols_T = sem("cols_T")
        cols_ready = sem("cols_ready")
        spread_done = sem("spread_done")
        masked = sem("masked")
        decay_ready = sem("decay_ready")
        angles = sem("angles")
        rope_ready = sem("rope_ready")
        tiles_done = sem("tiles_done")
        pair_ready = sem("pair_ready")
        gate_sig = sem("gate_sig")
        scores_done = sem("scores_done")
        probs_ready = sem("probs_ready")
        pv_done = sem("pv_done")
        den_ready = sem("den_ready")
        recip_ready = sem("recip_ready")
        y_ready = sem("y_ready")
        yT_done = sem("yT_done")
        mix_ready = sem("mix_ready")
        mix_hi = sem("mix_hi")
        mix_lo = sem("mix_lo")
        gate_normed = sem("gate_normed")
        silu_done = sem("silu_done")
        gate_scaled = sem("gate_scaled")
        rms_spread = sem("rms_spread")
        ff_ready = sem("ff_ready")
        ff_hi = sem("ff_hi")
        ff_lo = sem("ff_lo")
        stored = sem("stored")

        SMALL = 16 * 10
        CONSTS = 8
        V_HEADS = TT
        V_POST1 = V_HEADS + 2 * HEADS + 1
        V_NORM2 = V_POST1 + 1
        V_POST2 = V_NORM2 + 1
        Q_HEADS = TT
        Q_POST1 = Q_HEADS + TT * 2 * HEADS
        Q_NORM2 = Q_POST1 + 4 * TT
        Q_POST2 = Q_NORM2 + TT
        CHUNKS = 4
        OUT_PARTS = 2

        def pair_of(group, part, u):
            return 4 * group + 2 * part + u

        block = ctx.enter_context(nc.Block())

        @block.sync
        def _(sp):
            def load(rnd, q, src, wait=True):
                if wait:
                    sp.wait_ge(lo_done, 8 * (rnd - 1) + 2 * q + 2)
                k = src.shape[1]
                sp.dma_start(raw[:, q, :].rearrange("p (k c) -> p k c", k=k), src)\
                  .then_inc(raw_full[q], 16)

            def rows(w, k0, n, col, width):
                return w[k0 * P:(k0 + n) * P, bass.ds(col, width)].rearrange("(k p) c -> p k c", p=P)

            for t in range(TT):
                sp.dma_start(resid[:, t, :], x[0, t * P:(t + 1) * P, :]).then_inc(x_in[t], 16)
            for src, r0, n in ((g_mix_pre, C_GPRE, 16), (g_ffn_pre, C_GFFN, 16),
                               (conv_b, C_CONVB, 16), (g_mlstm_head, C_GHEAD, 8),
                               (g_ret_head, C_GHEAD + 8, 8)):
                sp.dma_start(right[r0:r0 + n, 0, 0:P], src[0, :].rearrange("(r c) -> r c", c=P))\
                  .then_inc(small_in, 16)
            sp.dma_start(right[C_CONVW:C_CONVW + 64, 0, 0:P],
                         conv_w[0].rearrange("j (r c) -> (j r) c", c=P)).then_inc(small_in, 16)
            sp.dma_start(vec[0:HEADS, 2:3], b_igate[0, :].rearrange("(h o) -> h o", o=1))\
              .then_inc(small_in, 16)
            sp.dma_start(vec[32:32 + HEADS, 2:3], b_fgate[0, :].rearrange("(h o) -> h o", o=1))\
              .then_inc(small_in, 16)
            sp.dma_start(vec[:, 0:1], inv_freq).then_inc(small_in, 16)
            sp.dma_start(cosT[:].bitcast(I32), positions[0:1, :].partition_broadcast(P))\
              .then_inc(small_in, 16)
            for r in range(4):
                for q in range(4):
                    col = 2 * DH + (r % 2) * 512 + (r // 2) * COL_RET
                    load(r, q, rows(w_in, 4 * q, 4, col, 512), wait=r > 0)
            with sp.Fori(0, 2) as kind:
                with sp.Fori(0, 2) as half:
                    for n, part in enumerate((0, 1, 3)):
                        for q in range(4):
                            col = COL_RET * kind + 512 * half + (part * DH + (q // 2) * 256)
                            load(6 * kind + 3 * half + (R_IN + n), q,
                                 rows(w_in, 8 * (q % 2), 8, col, 256))
            with sp.Fori(0, 4) as g:
                for q in range(4):
                    load(g + R_OUT, q, rows(w_out, 4 * q, 4, 512 * g, 512))
            with sp.Fori(0, PAIRS) as i:
                for q in range(4):
                    load(i + R_FF, q, rows(w_gate if q < 2 else w_up, 8 * (q % 2), 8, 256 * i, 256))
            for n in range(4 * KF // 4):
                g, k = divmod(n, KF // 4)
                load(R_DOWN + n // 4, n % 4, rows(w_down, 4 * k, 4, 512 * g, 512))
            for t in range(TT):
                for c in range(OUT_PARTS):
                    sp.wait_ge(resid_ready, TT * CHUNKS + OUT_PARTS * t + c + 1)
                    cols = slice(c * D // OUT_PARTS, (c + 1) * D // OUT_PARTS)
                    sp.dma_start(out[0, t * P:(t + 1) * P, cols], resid[:, t, cols]).then_inc(stored, 16)
            sp.wait_ge(stored, 16 * TT * OUT_PARTS)

        @block.gpsimd
        def _(pool):
            pool.memset(wg[:], 0.0).then_inc(zeroed, 1)
            pool.memset(ident, 0.0).then_inc(zeroed, 1)
            pool.memset(sel[:], 0.0).then_inc(zeroed, 1)
            pool.iota(rel[:, 0:2 * P], [[1, 2 * P]], base=0, channel_multiplier=-1,
                      allow_small_or_imprecise_dtypes=True).then_inc(zeroed, 1)
            pool.iota(rel[:, 2 * P:3 * P], [[1, P]], base=0, channel_multiplier=-1,
                      allow_small_or_imprecise_dtypes=True).then_inc(zeroed, 1)
            pool.wait_ge(zeroed, 5)
            pool.affine_select(ident, ident, [[-1, P]], ALU.not_equal, 1.0, base=0,
                               channel_multiplier=1).then_inc(consts, 1)
            pool.affine_select(sel[:], sel[:], [[-1, HEADS], [0, P]], ALU.not_equal, 1.0, base=0,
                               channel_multiplier=1).then_inc(consts, 1)
            for c in (0, 2):
                pool.affine_select(rel[:, c * P:(c + 1) * P], rel[:, c * P:(c + 1) * P], [[1, P]],
                                   ALU.is_ge, 1e9, base=0, channel_multiplier=-1).then_inc(consts, 1)
            pool.memset(pre[:, :, 0:CONV - 1], 0.0).then_inc(consts, 1)
            pool.memset(v_sb[:, :, 0:HEADS, HD:HD + 1], 1.0).then_inc(consts, 1)
            pool.memset(v_sb[:, :, HEADS:2 * HEADS, HD:HD + 1], 0.0).then_inc(consts, 1)
            pool.memset(floor[:, :, HEADS:2 * HEADS], 1.0).then_inc(consts, 1)
            pool.dma_start(wg[:, :, 0:HEADS], w_in[:, 4 * DH:4 * DH + HEADS].rearrange(
                "(k p) c -> p k c", p=P)).then_inc(wg_in, 16)
            pool.dma_start(wg[:, :, 32:32 + HEADS], w_in[:, 4 * DH + HEADS:COL_RET].rearrange(
                "(k p) c -> p k c", p=P)).then_inc(wg_in, 16)
            for h in range(HEADS):
                pool.wait_ge(decay_ready, HEADS + h + 1)
                for c in (0, 2):
                    block_ = decay[:, h, c * P:(c + 1) * P]
                    ins = pool.affine_select(block_, block_, [[1, P]], ALU.is_ge, 0.0, base=0,
                                             channel_multiplier=-1)
                ins.then_inc(masked, 1)
            pool.wait_ge(probs_ready, 2 * HEADS)
            pool.dma_start(g_post1[:], g_mix_post[0:1, :].partition_broadcast(P)).then_inc(post_in, 16)
            pool.wait_ge(sub_done, 8 * R_DOWN)
            pool.dma_start(g_post2[:], g_ffn_post[0:1, :].partition_broadcast(P)).then_inc(post_in, 16)

        @block.scalar
        def _(act):
            def square_root_table():
                act.activation(stat[:, S_SPARE + 1:S_SPARE + 2], stat[:, S_SPARE:S_SPARE + 1], ACT.Sqrt)

            def hi(rnd, s):
                rnd, s = rnd + s // 8, s % 8
                act.wait_ge(raw_full[s // 2], 16 * (rnd + 1))
                act.activation(w_hi[:, s % AHEAD, :], raw[:, s // 2, (s % 2) * SUB:(s % 2 + 1) * SUB],
                               ACT.Copy).then_inc(hi_done, 1)

            def ahead(rnd, s):
                act.wait_ge(sub_done, 8 * rnd + s + 1)
                hi(rnd, s + AHEAD)

            def root(dst, src, count):
                act.wait_ge(var_ready, count)
                act.activation(dst, src, ACT.Sqrt).then_inc(sd_ready, 1)

            def transposed_hi(dst, gain, banks0, tiles=range(KT)):
                for k in tiles:
                    act.wait_ge(xT_done, banks0 + k // 2 + 1)
                    act.activation(dst[:, k, 0:SEQ], bank[:, k // 2, (k % 2) * SEQ:(k % 2 + 1) * SEQ],
                                   ACT.Copy, scale=coef[:, gain + k:gain + k + 1]).then_inc(xT_hi, 1)

            act.wait_ge(acc_free, 2)
            square_root_table()
            for t in range(TT):
                act.wait_ge(x_in[t], 16)
                act.activation(h0[:, t, :], resid[:, t, :], ACT.Square,
                               accum_out=stat[:, S_SQ + t:S_SQ + t + 1]).then_inc(sq_done, 1)
                root(stat[:, S_SD + t:S_SD + t + 1], stat[:, S_VAR + t:S_VAR + t + 1], t + 1)
            hi(0, 0)
            act.wait_ge(coef_ready, 1)
            transposed_hi(hT, C_GPRE, 0, range(8))
            hi(0, 1)
            transposed_hi(hT, C_GPRE, 0, range(8, KT))
            hi(0, 2)
            hi(0, 3)

            def v_round(r, first=False):
                for s in range(8):
                    ahead(r, s)
                    if first and s == 0:
                        act.wait_ge(wg_in, 32)
                        act.activation(wg_hi[:], wg[:], ACT.Copy).then_inc(wg_rounded, 1)
                    if first and s in (2, 4):
                        n = s // 2 - 1
                        act.wait_ge(angles, n + 1)
                        act.activation((sinT, cosT)[n][:], row(2 + n), ACT.Sin,
                                       scale=1.0 if n else vec[:, 1:2]).then_inc(rope_ready, 1)
                    if first and s >= 6:
                        act.wait_ge(consts, CONSTS)
                        for h in range(4 * s - 24, 4 * s - 20):
                            act.activation(decay[:, HEADS + h, :], rel[:], ACT.Exp, scale=LOG_GAMMA[h])\
                               .then_inc(decay_ready, 1)

            v_round(0, first=True)
            with act.Fori(1, 4) as r:
                v_round(r)

            def mlstm_decay(h):
                if h % 2 == 0:
                    act.wait_ge(spread_done, h + 2)
                act.activation(decay[:, h, 0:SEQ], spread(h), ACT.Exp, bias=a_col[:, 0, h:h + 1])
                act.activation(decay[:, h, SEQ:3 * P], spread(h)[:, P:2 * P], ACT.Exp,
                               bias=a_col[:, 1, h:h + 1]).then_inc(decay_ready, 1)

            def copy_right(pair, event):
                act.wait_ge(acc_free, event + 2)
                act.activation(right[:], acc(pair)[:, :, SEQ:2 * SEQ], ACT.Copy)\
                   .then_inc(right_ready, 1)

            def head_col(a, c):
                return S_HEAD + S_HEAD_COLS * (a % 2) + c

            def head_stat(a, c):
                return stat[:, head_col(a, c):head_col(a, c) + 2]

            def head_step(rnd, s):
                a = head_at(rnd, s, 4)
                if a is not None:
                    root(head_stat(a, H_SD), head_stat(a, H_VAR), V_HEADS + a + 1)
                a = head_at(rnd, s, 3)
                if a is not None:
                    act.wait_ge(recip_ready, a + 1)
                    for t in range(TT):
                        if t:
                            act.wait_ge(sq_done, Q_HEADS + TT * a + t)
                        r, q = head_col(a, H_RECIP) + t, head_col(a, H_SQ) + t
                        act.activation(bank[:, B_PV + a % 2, 384:512], pv_out(a)[:, t, 0:HD],
                                       ACT.Square, scale=stat[:, r:r + 1],
                                       accum_out=stat[:, q:q + 1]).then_inc(sq_done, 1)
                a = head_at(rnd, s, 2)
                if a is not None:
                    act.wait_ge(pv_done, a + 1)
                    act.activation(head_stat(a, H_DEN), pv_out(a)[:, :, HD], ACT.Abs).then_inc(den_ready, 1)
                a = head_at(rnd, s, 7)
                if a is not None:
                    act.wait_ge(mix_ready, a + 1)
                    act.activation(mixT[:, a, 0:SEQ], gT[:, a % 4, :], ACT.Copy).then_inc(mix_hi, 1)

            def mixer_step(rnd, s):
                ended = unit_at(rnd, s, 0)
                if ended:
                    copy_right(ended[2], event_of(rnd, ended[2]))
                ended = unit_at(rnd, s, 1)
                if ended and ended[1] == 2:
                    group, part, u = ended
                    two = slice(2 * u, 2 * u + 2)
                    act.wait_ge(acc_free, event_of(gate_round(group), u) + 3)
                    act.activation(new if group >= 2 else gT[:, two, :], gT[:, two, :], ACT.Sigmoid)\
                       .then_inc(gate_sig, 1)
                ended = unit_at(rnd, s, 2)
                if ended and ended[1] < 2:
                    group, part, u = ended
                    act.wait_ge(tiles_done, pair_of(group, part, u) + 1)
                    act.activation((qT, kT)[part][:, 2 * u:2 * u + 2, :], new,
                                   ACT.Silu if group < 2 else ACT.Copy).then_inc(pair_ready, 1)

            def gate_rows():
                act.wait_ge(gates_full, 1)
                act.activation(row(R_RIGHT)[0:40], bank[0:40, 5, SEQ:2 * SEQ], ACT.Copy)\
                   .then_inc(gates_act, 1)
                act.wait_ge(gates_dve, 3)
                act.activation(row(R_EXP)[32:40], row(R_ABS)[32:40], ACT.Exp, scale=-1.0)\
                   .then_inc(gates_act, 1)
                act.wait_ge(gates_act, 2)
                act.activation(row(R_LN)[32:40], row(R_EXP)[32:40], ACT.Ln, bias=1.0)\
                   .then_inc(gates_act, 1)
                act.wait_ge(gates_dve, 10)
                act.activation(row(R_FLOOR)[0:HEADS], row(R_NEGROW)[0:HEADS], ACT.Exp)\
                   .then_inc(gates_act, 1)

            gate_rows()
            for rnd in range(R_IN, R_OUT):
                for s in range(8):
                    head_step(rnd, s)
                    ahead(rnd, s)
                    mixer_step(rnd, s)
                    if rnd == R_IN + 1 and 2 <= s < 5:
                        for h in range(3 * s - 6, min(3 * s - 3, HEADS)):
                            mlstm_decay(h)

            def squares(pair, subs, g, count):
                act.wait_ge(sub_done, subs)
                for t in range(TT):
                    act.wait_ge(sq_done, count + TT * g + t)
                    act.activation(bank[:, B_S, :], acc(pair)[:, t, :], ACT.Square,
                                   accum_out=stat[:, S_PSQ + 4 * t + g:S_PSQ + 4 * t + g + 1])\
                       .then_inc(sq_done, 1)

            for rnd in range(R_OUT, R_FF):
                for s in range(8):
                    head_step(rnd, s)
                    ahead(rnd, s)
                    mixer_step(rnd, s)
                if rnd == R_OUT:
                    square_root_table()
                squares(rnd % 2, 8 * rnd + 8, rnd - R_OUT, Q_POST1)

            root(stat[:, S_PSD:S_PSD + 2], stat[:, S_PVAR:S_PVAR + 2], V_POST1)
            for c in range(CHUNKS):
                transposed_hi(h2T, C_GFFN, KT // 2, range(4 * c, 4 * c + 4))

            def ffn_pair(i, first=False):
                for s in range(8):
                    ahead(i + R_FF, s)
                    if first and s < TT:
                        act.wait_ge(resid_ready, TT * CHUNKS)
                        act.activation(mixed[:, s, :], resid[:, s, :], ACT.Square,
                                       accum_out=stat[:, S_SQ + s:S_SQ + s + 1]).then_inc(sq_done, 1)
                    if first and s == 2:
                        root(stat[:, S_SD:S_SD + 2], stat[:, S_VAR:S_VAR + 2], V_NORM2)
                    if s == 3:
                        copy_right(0, 2 * i + E_FF)
                    if s == (6 if first else 4):
                        act.wait_ge(gate_normed, i + 1)
                        act.activation(ff_g[:], ff_g[:], ACT.Silu).then_inc(silu_done, 1)
                    if s == 7:
                        copy_right(1, 2 * i + (E_FF + 1))
                        act.wait_ge(ff_ready, i + 1)
                        act.activation(ffT[:, bass.ds(2 * i, 2), 0:SEQ], ff_u[:], ACT.Copy)\
                           .then_inc(ff_hi, 1)

            ffn_pair(0, first=True)
            with act.Fori(1, PAIRS) as i:
                ffn_pair(i)

            square_root_table()
            for n in range(4 * DOWN_SUBS):
                if 8 * R_DOWN + n + AHEAD < N_SUBS:
                    ahead(R_DOWN, n)
                g, s = divmod(n, DOWN_SUBS)
                if s == DOWN_SUBS - 1:
                    squares(g % 2, 8 * R_DOWN + n + 1, g, Q_POST2)
            root(stat[:, S_PSD:S_PSD + 2], stat[:, S_PVAR:S_PVAR + 2], V_POST2)

        @block.vector
        def _(dve):
            steps = [0]

            def link(ins):
                steps[0] += 1
                ins.then_inc(dve_step, 1)
                dve.wait_ge(dve_step, steps[0])

            def lo(rnd, s):
                rnd, s = rnd + s // 8, s % 8
                dve.wait_ge(hi_done, 8 * rnd + s + 1)
                dve.tensor_tensor(w_lo[:, s % AHEAD, :], raw[:, s // 2, (s % 2) * SUB:(s % 2 + 1) * SUB],
                                  w_hi[:, s % AHEAD, :].bitcast(F32), ALU.subtract).then_inc(lo_done, 1)

            def transposed_lo(dst, gain, tiles0, tiles=range(KT)):
                for k in tiles:
                    dve.wait_ge(xT_hi, tiles0 + 2 * (k // 2) + 2)
                    dve.scalar_tensor_tensor(
                        dst[:, k, SEQ:2 * SEQ], bank[:, k // 2, (k % 2) * SEQ:(k % 2 + 1) * SEQ],
                        coef[:, gain + k:gain + k + 1], dst[:, k, 0:SEQ].bitcast(F32),
                        ALU.mult, ALU.subtract).then_inc(xT_lo, 1)

            dve.memset(vec[0:64, 1:2], 1.0)
            dve.memset(vec[64:128, 1:2], -1.0)
            dve.memset(stat[:, S_SPARE:S_SPARE + 1], 0.0).then_inc(acc_free, 2)
            dve.memset(stat[:, S_SPARE + 2:S_SPARE + 3], 0.0).then_inc(y_ready, 2)
            for t in range(TT):
                dve.wait_ge(sq_done, t + 1)
                dve.tensor_scalar(stat[:, S_VAR + t:S_VAR + t + 1], stat[:, S_SQ + t:S_SQ + t + 1],
                                  1.0 / D, EPS, ALU.mult, ALU.add).then_inc(var_ready, 1)
                dve.wait_ge(sd_ready, t + 1)
                link(dve.reciprocal(stat[:, S_RSTD + t:S_RSTD + t + 1], stat[:, S_SD + t:S_SD + t + 1]))
                dve.tensor_scalar(h0[:, t, :], resid[:, t, :], stat[:, S_RSTD + t:S_RSTD + t + 1],
                                  None, ALU.mult).then_inc(h_ready, 1)
            dve.wait_ge(coef_T, 1)
            dve.tensor_copy(coef, bank[:, 7, 0:P]).then_inc(coef_ready, 1)
            lo(0, 0)
            dve.wait_ge(coef_ready, 1)
            transposed_lo(hT, C_GPRE, 0, range(8))
            lo(0, 1)
            transposed_lo(hT, C_GPRE, 0, range(8, KT))
            lo(0, 2)
            lo(0, 3)

            pos, ang, turns = row(0), row(1), row(4)

            def angle(dst, quarter):
                link(dve.tensor_scalar(turns, ang, 1.0 / (2 * math.pi), quarter, ALU.mult, ALU.add))
                link(dve.tensor_scalar(turns, turns, ROUND, None, ALU.add))
                link(dve.tensor_scalar(turns, turns, ROUND, quarter, ALU.subtract, ALU.subtract))
                link(dve.scalar_tensor_tensor(dst, turns, -TWO_PI_1, ang, ALU.mult, ALU.add))
                link(dve.scalar_tensor_tensor(dst, turns, -TWO_PI_2, dst, ALU.mult, ALU.add))
                link(dve.scalar_tensor_tensor(dst, turns, -TWO_PI_3, dst, ALU.mult, ALU.add))
                dve.tensor_scalar(dst, dst, -3.1415925, 3.1415925, ALU.max, ALU.min).then_inc(angles, 1)

            def v_rounds(i, first=False):
                for e in range(2):
                    for s in range(8):
                        lo(2 * i + e, s + AHEAD)
                        if first and e == 0 and s == 0:
                            dve.wait_ge(small_in, SMALL)
                            link(dve.tensor_copy(pos, cosT[:].bitcast(I32)))
                            link(dve.tensor_scalar(ang, pos, vec[:, 0:1], None, ALU.mult))
                            angle(row(2), 0.0)
                        if first and e == 0 and s == 2:
                            angle(row(3), 0.25)
                        if first and e == 0 and s == 4:
                            dve.wait_ge(wg_rounded, 1)
                            dve.tensor_tensor(wg_lo[:], wg[:], wg_hi[:].bitcast(F32), ALU.subtract)\
                               .then_inc(wg_ready, 1)
                    dve.wait_ge(sub_done, 16 * i + (8 * e + 8))
                    for t in range(TT):
                        ins = dve.tensor_copy(v_sb[:, t, bass.ds(8 * i + 4 * e, 4), 0:HD],
                                              acc(e)[:, t, :].rearrange("p (h c) -> p h c", c=HD))
                    ins.then_inc(acc_free, 1)

            v_rounds(0, first=True)
            v_rounds(1)

            def gates(ins, n):
                ins.then_inc(gates_dve, 1)
                dve.wait_ge(gates_dve, n)

            def rowi(n):
                return row(n)[0:HEADS]

            def rowf(n):
                return row(n)[32:32 + HEADS]

            dve.wait_ge(rope_ready, 2)
            dve.wait_ge(gates_act, 1)
            for n, p0 in enumerate((0, 32)):
                gates(dve.scalar_tensor_tensor(row(R_Z)[p0:p0 + HEADS], bank[p0:p0 + HEADS, 5, 0:SEQ],
                                               vec[p0:p0 + HEADS, 2:3], row(R_RIGHT)[p0:p0 + HEADS],
                                               ALU.add, ALU.add), n + 1)
            gates(dve.scalar_tensor_tensor(rowf(R_ABS), rowf(R_Z), -1.0, rowf(R_Z), ALU.mult, ALU.max), 3)
            link(dve.memset(rowf(R_ONES), 1.0))
            dve.wait_ge(gates_act, 3)
            gates(dve.scalar_tensor_tensor(rowf(R_A), rowf(R_Z), 0.0, rowf(R_LN), ALU.min, ALU.subtract), 4)
            gates(dve.tensor_tensor_scan(rowf(R_F), rowf(R_ONES), rowf(R_A), 0.0, ALU.mult, ALU.add), 5)
            gates(dve.tensor_copy(rowi(R_F), rowf(R_F)), 6)
            gates(dve.tensor_tensor(rowi(R_A), rowi(R_Z), rowi(R_F), ALU.subtract), 7)
            gates(dve.tensor_tensor_scan(rowi(R_M), rowi(R_A), rowi(R_A), 0.0, ALU.max, ALU.max), 8)
            gates(dve.tensor_scalar(rowi(R_NEGM), rowi(R_M), -1.0, None, ALU.mult), 9)
            gates(dve.scalar_tensor_tensor(rowi(R_NEGROW), rowi(R_F), -1.0, rowi(R_M), ALU.mult,
                                           ALU.subtract), 10)

            def gate_columns():
                dve.wait_ge(cols_T, 1)
                cols = bank[:, 4, 0:4 * HEADS].rearrange("p (n t h) -> p n t h", n=2, t=TT)
                dve.tensor_copy(a_col[:], cols[:, 0])
                dve.wait_ge(consts, CONSTS)
                dve.tensor_copy(floor[:, :, 0:HEADS], cols[:, 1]).then_inc(cols_ready, 1)

            def unit_sums(rnd, u, part):
                event = event_of(rnd, u)
                dve.wait_ge(right_ready, event - E_IN + 1)
                summed = gT[:, 2 * u:2 * u + 2, :] if part == 2 else new
                dve.tensor_tensor(summed, acc(u)[:, :, 0:SEQ], right[:], ALU.add).then_inc(acc_free, 1)
                dve.wait_ge(acc_free, event + 3)

            def signalled(ins):
                steps[0] += 1
                ins.then_inc(dve_step, 1)
                return steps[0]

            conv_step = [0, 0]

            def convolve(group, part, u, half):
                for j in (2 * half, 2 * half + 1):
                    for c in range(2):
                        n = HEADS * part + 4 * group + 2 * u + c
                        tap = coef[:, C_CONVW + 16 * j + n:C_CONVW + 16 * j + n + 1]
                        src, work = pre[:, c, j:j + SEQ], spin[:, c, :]
                        if j == 0:
                            ins = dve.tensor_scalar(work, src, tap, coef[:, C_CONVB + n:C_CONVB + n + 1],
                                                    ALU.mult, ALU.add)
                        else:
                            dve.wait_ge(dve_step, conv_step[c])
                            ins = dve.scalar_tensor_tensor(work if j < CONV - 1 else new[:, c, :], src,
                                                           tap, work, ALU.mult, ALU.add)
                        conv_step[c] = signalled(ins) if j < CONV - 1 else 0
                if half:
                    ins.then_inc(tiles_done, 1)

            def rotate(group, part, u, half):
                if half == 0:
                    for p0, p1 in ((0, 64), (64, 0)):
                        ins = dve.tensor_tensor(spin[p0:p0 + 64], new[p1:p1 + 64],
                                                two(sinT[p1:p1 + 64, :], 64), ALU.mult)
                    link(ins)
                    conv_step[0] = signalled(dve.tensor_tensor(new, new, two(cosT[:], P), ALU.mult))
                else:
                    dve.wait_ge(dve_step, conv_step[0])
                    dve.tensor_tensor(new, new, spin, ALU.add).then_inc(tiles_done, 1)

            def two(table, rows):
                return table.unsqueeze(1).to_broadcast([rows, 2, SEQ])

            def weigh(a):
                dve.wait_ge(scores_done, a + 1)
                dve.wait_ge(*((masked, a + 1) if a < HEADS else (decay_ready, HEADS)))
                if a >= 1:
                    dve.wait_ge(pv_done, a)
                dve.scalar_tensor_tensor(probs[:], bank[:, B_S, 0:3 * P], SCALE, decay[:, a, :],
                                         ALU.mult, ALU.mult).then_inc(probs_ready, 1)

            def head_stat(a, c):
                c += S_HEAD + S_HEAD_COLS * (a % 2)
                return stat[:, c:c + 2]

            def head_recip(a):
                dve.wait_ge(den_ready, a + 1)
                link(dve.tensor_tensor(head_stat(a, H_DEN), head_stat(a, H_DEN), floor[:, :, a], ALU.max))
                dve.reciprocal(head_stat(a, H_RECIP), head_stat(a, H_DEN)).then_inc(recip_ready, 1)

            def head_variance(a):
                dve.wait_ge(sq_done, Q_HEADS + TT * (a + 1))
                dve.tensor_scalar(head_stat(a, H_VAR), head_stat(a, H_SQ), 1.0 / HD, EPS, ALU.mult,
                                  ALU.add).then_inc(var_ready, 1)

            def head_scaled(a):
                dve.wait_ge(sd_ready, V_HEADS + a + 1)
                link(dve.reciprocal(head_stat(a, H_RSTD), head_stat(a, H_SD)))
                link(dve.tensor_tensor(head_stat(a, H_SCALE), head_stat(a, H_RSTD),
                                       head_stat(a, H_RECIP), ALU.mult))
                if a >= 2:
                    dve.wait_ge(yT_done, a - 1)
                for t in range(TT):
                    ins = dve.tensor_scalar(y[:, a % 2, t, :], pv_out(a)[:, t, 0:HD],
                                            head_stat(a, H_SCALE)[:, t:t + 1], None, ALU.mult)
                ins.then_inc(y_ready, 1)

            def mix(a):
                dve.wait_ge(yT_done, a + 1)
                dve.wait_ge(gate_sig, a // 2 + 1)
                dve.scalar_tensor_tensor(gT[:, a % 4, :], bank[:, B_T, 0:SEQ],
                                         coef[:, C_GHEAD + a:C_GHEAD + a + 1], gT[:, a % 4, :],
                                         ALU.mult, ALU.mult).then_inc(mix_ready, 1)

            def mix_rest(a):
                dve.wait_ge(mix_hi, a + 1)
                dve.tensor_tensor(mixT[:, a, SEQ:2 * SEQ], gT[:, a % 4, :],
                                  mixT[:, a, 0:SEQ].bitcast(F32), ALU.subtract).then_inc(mix_lo, 1)

            def head_step(rnd, s):
                for step, first in ((weigh, 0), (mix, 6), (head_scaled, 4), (head_variance, 3),
                                    (head_recip, 2), (mix_rest, 8)):
                    a = head_at(rnd, s, first)
                    if a is not None:
                        step(a)

            def mixer_step(rnd, s):
                for half in (1, 0):
                    ended = unit_at(rnd, s, half)
                    if ended:
                        group, part, u = ended
                        if half == 0:
                            unit_sums(rnd, u, part)
                        if part < 2:
                            (convolve if group < 2 else rotate)(group, part, u, half)
                ended = unit_at(rnd, s, 2)
                if ended and ended[0] >= 2 and ended[1] == 2:
                    group, part, u = ended
                    dve.wait_ge(gate_sig, 2 * group + u + 1)
                    link(dve.tensor_tensor(gT[:, 2 * u:2 * u + 2, :], gT[:, 2 * u:2 * u + 2, :], new,
                                           ALU.mult))

            for rnd in range(R_IN, R_OUT):
                for s in range(8):
                    head_step(rnd, s)
                    lo(rnd, s + AHEAD)
                    mixer_step(rnd, s)
                    if rnd == R_IN and s == 5:
                        gate_columns()

            def emptied(pair, dst, gain, g, squares0):
                for t in range(TT):
                    dve.wait_ge(sq_done, squares0 + TT * g + t + 1)
                    ins = dve.tensor_tensor(dst[:, t, 512 * g:512 * (g + 1)], acc(pair)[:, t, :],
                                            gain[:, 512 * g:512 * (g + 1)], ALU.mult)
                ins.then_inc(acc_free, 1)

            def result_norm(acc_count, sd_count):
                link(dve.tensor_reduce(stat[:, S_PSUM:S_PSUM + 2],
                                       stat[:, S_PSQ:S_PSQ + 8].rearrange("p (t g) -> p t g", t=TT),
                                       mybir.AxisListType.X, ALU.add))
                dve.tensor_scalar(stat[:, S_PVAR:S_PVAR + 2], stat[:, S_PSUM:S_PSUM + 2],
                                  1.0 / D, EPS, ALU.mult, ALU.add).then_inc(var_ready, 1)
                dve.wait_ge(sd_ready, sd_count)
                link(dve.reciprocal(stat[:, S_PRSTD:S_PRSTD + 2], stat[:, S_PSD:S_PSD + 2]))
                dve.wait_ge(acc_free, acc_count)

            def add_result(src, t, c0, c1):
                dve.scalar_tensor_tensor(resid[:, t, c0:c1], src[:, t, c0:c1],
                                         stat[:, S_PRSTD + t:S_PRSTD + t + 1], resid[:, t, c0:c1],
                                         ALU.mult, ALU.add).then_inc(resid_ready, 1)

            for rnd in range(R_OUT, R_FF):
                g = rnd - R_OUT
                for s in range(8):
                    head_step(rnd, s)
                    lo(rnd, s + AHEAD)
                    mixer_step(rnd, s)
                if g == 0:
                    dve.wait_ge(post_in, 16)
                emptied(rnd % 2, mixed, g_post1, g, Q_POST1)
            result_norm(E_FF + 2, V_POST1)
            for c in range(CHUNKS + 1):
                if c < CHUNKS:
                    for t in range(TT):
                        add_result(mixed, t, 512 * c, 512 * (c + 1))
                if c:
                    transposed_lo(h2T, C_GFFN, KT, range(4 * c - 4, 4 * c))

            def token_norms_a():
                dve.wait_ge(sq_done, Q_NORM2 + TT)
                dve.tensor_scalar(stat[:, S_VAR:S_VAR + 2], stat[:, S_SQ:S_SQ + 2], 1.0 / D, EPS,
                                  ALU.mult, ALU.add).then_inc(var_ready, 1)
                dve.wait_ge(sd_ready, V_NORM2)
                link(dve.reciprocal(stat[:, S_RSTD:S_RSTD + 2], stat[:, S_SD:S_SD + 2]))
                for t in range(TT):
                    link(dve.memset(ff_u[:, 0, t * P:(t + 1) * P], 1.0))
                    dve.tensor_scalar(ff_u[:, 0, t * P:(t + 1) * P], ff_u[:, 0, t * P:(t + 1) * P],
                                      stat[:, S_RSTD + t:S_RSTD + t + 1], None, ALU.mult)\
                       .then_inc(h_ready, 1)

            def token_norms_b():
                dve.wait_ge(rms_spread, 1)
                link(dve.tensor_copy(rms_row, bank[:, B_S, 0:SEQ]))

            def ffn_pair(i, first=False):
                for s in range(8):
                    lo(i + R_FF, s + AHEAD)
                    if first and s == 2:
                        token_norms_a()
                    if s == 3:
                        dve.wait_ge(right_ready, 2 * i + (E_OUT - E_IN + 1))
                        dve.tensor_tensor(ff_g[:], acc(0)[:, :, 0:SEQ], right[:], ALU.add)\
                           .then_inc(acc_free, 1)
                    if first and s == 5:
                        token_norms_b()
                    if s == (5 if first else 3):
                        dve.wait_ge(acc_free, 2 * i + (E_FF + 3))
                        dve.tensor_tensor(ff_g[:], ff_g[:], rms2, ALU.mult).then_inc(gate_normed, 1)
                    if s == (7 if first else 5):
                        dve.wait_ge(silu_done, i + 1)
                        dve.tensor_tensor(ff_g[:], ff_g[:], rms2, ALU.mult).then_inc(gate_scaled, 1)
                    if s == 7:
                        dve.wait_ge(right_ready, 2 * i + (E_OUT - E_IN + 2))
                        dve.tensor_tensor(ff_u[:], acc(1)[:, :, 0:SEQ], right[:], ALU.add)\
                           .then_inc(acc_free, 1)
                        dve.wait_ge(acc_free, 2 * i + (E_FF + 4))
                        dve.wait_ge(gate_scaled, i + 1)
                        dve.tensor_tensor(ff_u[:], ff_u[:], ff_g[:], ALU.mult).then_inc(ff_ready, 1)
                        dve.wait_ge(ff_hi, i + 1)
                        dve.tensor_tensor(ffT[:, bass.ds(2 * i, 2), SEQ:2 * SEQ], ff_u[:],
                                          ffT[:, bass.ds(2 * i, 2), 0:SEQ].bitcast(F32), ALU.subtract)\
                           .then_inc(ff_lo, 1)

            rms2 = rms_row.unsqueeze(1).to_broadcast([P, 2, SEQ])
            ffn_pair(0, first=True)
            with dve.Fori(1, PAIRS) as i:
                ffn_pair(i)

            for n in range(4 * DOWN_SUBS):
                if 8 * R_DOWN + n + AHEAD < N_SUBS:
                    lo(R_DOWN, n + AHEAD)
                g, s = divmod(n, DOWN_SUBS)
                if s == DOWN_SUBS - 1:
                    if g == 0:
                        dve.wait_ge(post_in, 32)
                    emptied(g % 2, ff_out, g_post2, g, Q_POST2)
            result_norm(E_DOWN + 4 + 2, V_POST2)
            for t in range(TT):
                for c in range(OUT_PARTS):
                    add_result(ff_out, t, c * D // OUT_PARTS, (c + 1) * D // OUT_PARTS)

        @block.tensor
        def _(pe):
            def mm(out_, lhsT, rhs, start, stop):
                return pe.matmul(out_, lhsT, rhs, start=start, stop=stop, skip_group_check=True)

            def transposed(src, t, b):
                for k in range(2):
                    ins = pe.transpose(bank[:, b, k * SEQ + t * P:k * SEQ + (t + 1) * P],
                                       src[:, t, (2 * b + k) * P:(2 * b + k + 1) * P], ident)
                if t == TT - 1:
                    ins.then_inc(xT_done, 1)

            def sub_columns(rnd, s, act_T, pair):
                pe.wait_ge(lo_done, 8 * rnd + s + 1)
                slot, quarter = s % AHEAD, s % 4
                for c in range(2):
                    for j in range(4):
                        k = 4 * quarter + j
                        cols = slice(256 * j + P * c, 256 * j + P * (c + 1))
                        mm(bank[:, 2 * pair + c, :], w_hi[:, slot, cols], act_T[:, k, :], k == 0, False)
                        ins = mm(bank[:, 2 * pair + c, 0:SEQ], w_lo[:, slot, cols], act_T[:, k, 0:SEQ],
                                 False, k == KT - 1)
                ins.then_inc(sub_done, 1)

            def unit_columns(rnd, unit, event, act_T, before=None, after=None):
                pe.wait_ge(acc_free, event + 1)
                for q in range(4):
                    s = 4 * unit + q
                    if before:
                        before(s)
                    sub_columns(rnd, s, act_T, unit)
                    if after:
                        after(s)

            def sub_tokens(count, slot, act_T, pair, k0, last):
                pe.wait_ge(lo_done, count)
                for j in range(2):
                    k, w = k0 + j, slice(512 * j, 512 * (j + 1))
                    for t in range(TT):
                        hi_x = act_T[:, k, t * P:(t + 1) * P]
                        lo_x = act_T[:, k, SEQ + t * P:SEQ + (t + 1) * P]
                        mm(bank[:, 2 * pair + t, :], hi_x, w_hi[:, slot, w], k == 0, False)
                        mm(bank[:, 2 * pair + t, :], hi_x, w_lo[:, slot, w], False, False)
                        ins = mm(bank[:, 2 * pair + t, :], lo_x, w_hi[:, slot, w], False, k == last)
                ins.then_inc(sub_done, 1)

            def keep_clock(products, b):
                for _ in range(products):
                    mm(bank[:, b, 0:P], ident, ident, True, True)

            pe.wait_ge(consts, 1)
            keep_clock(17, 6)
            pe.wait_ge(small_in, SMALL)
            pe.transpose(bank[:, 7, 0:P], right[:, 0, 0:P], ident).then_inc(coef_T, 1)
            for t in range(TT):
                pe.wait_ge(h_ready, t + 1)
                for b in range(KT // 2):
                    if b == 7 and t == 0:
                        pe.wait_ge(coef_ready, 1)
                    transposed(h0, t, b)

            with pe.Fori(0, 2) as i:
                for e in range(2):
                    pe.wait_ge(acc_free, 2 * i + (e + 1))
                    for s in range(8):
                        pe.wait_ge(xT_lo, max(2 * s + 2, 4))
                        sub_tokens(16 * i + (8 * e + s + 1), s % AHEAD, hT, e, 2 * s, KT - 1)

            pe.wait_ge(wg_ready, 1)
            for k in range(KT):
                mm(bank[0:40, 5, :], wg_hi[:, k, :], hT[:, k, :], k == 0, False)
                ins = mm(bank[0:40, 5, 0:SEQ], wg_lo[:, k, :], hT[:, k, 0:SEQ], False, k == KT - 1)
            ins.then_inc(gates_full, 1)

            def gate_columns():
                pe.wait_ge(gates_act, 4)
                pe.wait_ge(gates_dve, 10)
                for n, r in enumerate((R_A, R_FLOOR)):
                    for t in range(TT):
                        c = (TT * n + t) * HEADS
                        ins = pe.transpose(bank[:, 4, c:c + HEADS], row(r)[0:HEADS, t * P:(t + 1) * P],
                                           ident[0:HEADS, 0:HEADS])
                ins.then_inc(cols_T, 1)

            def spread_rows():
                pe.wait_ge(consts, CONSTS)
                pe.wait_ge(cols_ready, 1)
                for h in range(HEADS):
                    mm(spread(h), sel[:, h, :], row(R_NEGM)[0:HEADS], True, True)\
                        .then_inc(spread_done, 1)

            def scores(group, n):
                pe.wait_ge(decay_ready, 2 * HEADS)
                pe.wait_ge(pair_ready, 4 * group + (3 + n // 2))
                mm(bank[:, B_S, 0:SEQ], kT[:, n, 0:P], qT[:, n, :], True, True)
                mm(bank[:, B_S, SEQ:SEQ + P], kT[:, n, P:2 * P], qT[:, n, P:2 * P], True, True)\
                    .then_inc(scores_done, 1)

            def weighted(group, n):
                pe.wait_ge(probs_ready, 4 * group + (n + 1))
                pe.wait_ge(y_ready, 4 * group + (n + 1))
                o = bank[:, B_PV + n % 2, :]
                v = v_sb[:, :, bass.ds(4 * group + n, 1), :].rearrange("p t o c -> p t (o c)")
                mm(o[:, 0:HD + 1], probs[:, 0:P], v[:, 0, :], True, True)
                mm(o[:, HD + 1:2 * (HD + 1)], probs[:, P:2 * P], v[:, 0, :], False, False)
                mm(o[:, HD + 1:2 * (HD + 1)], probs[:, 2 * P:3 * P], v[:, 1, :], False, True)\
                    .then_inc(pv_done, 1)

            def turned(group, n):
                pe.wait_ge(y_ready, 4 * group + (n + 3))
                if n:
                    pe.wait_ge(mix_ready, 4 * group + n)
                for t in range(TT):
                    ins = pe.transpose(bank[:, B_T, t * P:(t + 1) * P], y[:, n % 2, t, :], ident)
                ins.then_inc(yT_done, 1)

            def gate_units(group, rnd, event):
                def before(s):
                    if s % 2 == 0:
                        scores(group, s // 2)

                def after(s):
                    if s % 2 == 1:
                        weighted(group, s // 2)
                        if s >= 5:
                            turned(group, (s - 5) // 2)

                for u in range(2):
                    unit_columns(rnd, u, event + u, hT, before, after)

            def left_over(group):
                return lambda s: turned(group, 2 + s // 2) if s in (1, 3) else None

            unit_columns(R_IN, 0, event_of(R_IN, 0), hT)
            unit_columns(R_IN, 1, event_of(R_IN, 1), hT,
                         after=lambda s: gate_columns() if s == 5 else spread_rows() if s == 7 else None)
            for u in range(2):
                unit_columns(R_IN + 1, u, event_of(R_IN + 1, u), hT)
            with pe.Fori(0, 3) as j:
                gate_units(j, 3 * j + gate_round(0), 6 * j + event_of(gate_round(0), 0))
                for n in (1, 2):
                    for u in range(2):
                        unit_columns(3 * j + (gate_round(0) + n), u,
                                     6 * j + event_of(gate_round(0) + n, u), hT,
                                     after=left_over(j) if n == 1 else None)
            gate_units(3, gate_round(3), event_of(gate_round(3), 0))

            for g in range(4):
                pe.wait_ge(acc_free, E_OUT + g + 1)
                for s in range(8):
                    if g == 0:
                        pe.wait_ge(mix_lo, 2 * s + 2)
                    sub_tokens(8 * (R_OUT + g) + s + 1, s % AHEAD, mixT, g % 2, 2 * s, KT - 1)
                    if g == 0:
                        left_over(3)(s)

            def chunk_transposed(c):
                pe.wait_ge(resid_ready, TT * (c + 1))
                for b in (2 * c, 2 * c + 1):
                    for t in range(TT):
                        transposed(resid, t, b)

            def first_pair(s):
                if s < 4:
                    pe.wait_ge(xT_lo, KT + 4 * (s + 1))

            def first_pair_after(s):
                if s < 2:
                    chunk_transposed(s + 2)
                if s == 5:
                    pe.wait_ge(h_ready, 2 * TT)
                    for t in range(TT):
                        ins = mm(bank[:, B_S, t * P:(t + 1) * P], ff_u[:, 0, t * P:(t + 1) * P], ident,
                                 True, True)
                    ins.then_inc(rms_spread, 1)

            keep_clock(20, 7)
            chunk_transposed(0)
            chunk_transposed(1)
            for u in range(2):
                unit_columns(R_FF, u, E_FF + u, h2T, first_pair, first_pair_after)
            with pe.Fori(1, PAIRS) as i:
                for u in range(2):
                    unit_columns(i + R_FF, u, 2 * i + (E_FF + u), h2T)

            for g in range(4):
                pe.wait_ge(acc_free, E_DOWN + g + 1)
                for s in range(DOWN_SUBS):
                    n = DOWN_SUBS * g + s
                    if g == 0:
                        pe.wait_ge(ff_lo, s + 1)
                    sub_tokens(8 * R_DOWN + n + 1, n % AHEAD, ffT, g % 2, 2 * s, KF - 1)


_INS = ["x", "positions", "g_mix_pre", "w_in", "conv_w", "conv_b", "b_igate", "b_fgate",
        "g_mlstm_head", "g_ret_head", "w_out", "g_mix_post", "g_ffn_pre", "w_gate", "w_up", "w_down",
        "g_ffn_post"]


def kernel(**inputs):
    import concourse.bacc as bacc
    from concourse.bass_utils import run_bass_kernel_spmd

    nc = bacc.Bacc("TRN2", target_bir_lowering=False, num_devices=1)
    arrays, args = {}, []
    steps = np.arange(0, HD, 2, dtype=np.float32) / np.float32(HD)
    inv_freq = np.power(np.float32(10000.0), -steps).astype(np.float32)
    constants = {"inv_freq": np.concatenate([inv_freq, inv_freq]).reshape(P, 1)}
    for name in _INS + ["inv_freq"]:
        a = np.ascontiguousarray(constants[name] if name in constants else inputs[name])
        if a.ndim == 3 and a.shape[0] == 1 and name.startswith("w_"):
            a = a[0]
        arrays[f"in_{name}"] = a
        args.append(nc.dram_tensor(f"in_{name}", a.shape, mybir.dt.from_np(a.dtype),
                                   kind="ExternalInput").ap())
    out = nc.dram_tensor("out_0", (1, SEQ, D), F32, kind="ExternalOutput").ap()
    hybrid_layer(nc, *args, out)
    r = run_bass_kernel_spmd(nc, [arrays], core_ids=[0])
    return r.results[0]["out_0"]
```

```python
import math
from contextlib import ExitStack

import numpy as np

import concourse.bass as bass
from concourse import mybir

ALU = mybir.AluOpType
ACT = mybir.ActivationFunctionType
F32 = mybir.dt.float32
F32R = mybir.dt.float32r
I32 = mybir.dt.int32

P = 128
SEQ = 256
D = 2048
HD = 128
HEADS = 8
DH = HEADS * HD
D_FF = 5632
KT = D // P
KF = D_FF // P
TT = SEQ // P
CONV = 4
EPS = 1e-6
SCALE = HD ** -0.5
COL_RET = 4 * DH + 2 * HEADS

SUB = 1024
RAW_CHUNKS = 4
AHEAD = 4
R_V = 0
R_IN = R_V + 4
R_OUT = R_IN + 12
R_FF = R_OUT + 4
PAIRS = D_FF // 256
R_DOWN = R_FF + PAIRS
DOWN_SUBS = KF // 2
N_SUBS = 8 * R_DOWN + 4 * DOWN_SUBS
SPLIT_OUT = 2
E_IN = 4
E_OUT = E_IN + 24
E_FF = E_OUT + 4
E_DOWN = E_FF + 2 * PAIRS
C_GPRE, C_GFFN, C_CONVB, C_GHEAD, C_CONVW = 0, 16, 32, 48, 64

TWO_PI_1 = 6.28125
TWO_PI_2 = float(np.float32(np.float64(2 * np.pi - 6.28125).astype(np.float16)))
TWO_PI_3 = float(np.float32(2 * np.pi - 6.28125 - TWO_PI_2))
ROUND = 1.5 * 2.0 ** 23
LOG_GAMMA = [math.log(1.0 - 2.0 ** (-5.0 - h)) for h in range(HEADS)]


S_SQ, S_VAR, S_SD, S_RSTD = 0, 2, 4, 6
S_PSQ, S_PSUM, S_PVAR, S_PSD, S_PRSTD = 8, 16, 18, 20, 22
S_SPARE = 24
S_HEAD, S_HEAD_COLS = 32, 16
H_DEN, H_RECIP, H_SQ, H_VAR, H_SD, H_RSTD, H_SCALE = range(0, 14, 2)


def event_of(rnd, unit):
    return 2 * rnd - 4 + unit


def gate_round(group):
    return R_IN + 3 * group + 2


def start_tiles(s):
    return {0: range(4), 2: range(4, 8), AHEAD: range(8, KT)}.get(s, ())


def head_at(rnd, s, first):
    for group in range(4):
        n, odd = divmod(8 * (rnd - gate_round(group)) + s - first, 2)
        if not odd and 0 <= n < 4:
            return 4 * group + n
    return None


def unit_at(rnd, s, lag):
    rnd, s = rnd - (lag > s), (s - lag) % 8
    if R_IN <= rnd < R_OUT and s % 4 == 3:
        return (*divmod(rnd - R_IN, 3), s // 4)
    return None


def hybrid_layer(nc, x, positions, g_mix_pre, w_in, conv_w, conv_b, b_igate, b_fgate, g_mlstm_head,
                 g_ret_head, w_out, g_mix_post, g_ffn_pre, w_gate, w_up, w_down, g_ffn_post,
                 inv_freq, out):
    with ExitStack() as ctx:
        def sb(name, shape, dt=F32, stack=ctx):
            return stack.enter_context(nc.sbuf_tensor(name, shape, dt))

        def sem(name):
            return ctx.enter_context(nc.semaphore(name))

        raw = sb("raw", [P, RAW_CHUNKS, 2 * SUB])
        w_hi = sb("w_hi", [P, AHEAD, SUB], F32R)
        w_lo = sb("w_lo", [P, AHEAD, SUB], F32R)
        resid = sb("resid", [P, TT, D])
        columns = sb("columns", [P, 2, P])
        ident, coef = columns[:, 0, :], columns[:, 1, :]
        rms_row = columns[:].rearrange("p a c -> p (a c)")
        right = sb("right", [P, 2, SEQ])
        stat = sb("stat", [P, S_HEAD + 2 * S_HEAD_COLS])

        mixer = ExitStack()
        late = ExitStack()
        mixed = sb("mixed", [P, TT, D], stack=late)
        g_post1 = sb("g_post1", [P, D], stack=late)
        late.close()
        decay = sb("decay", [P, 2 * HEADS, 3 * P], stack=mixer)
        v_sb = sb("v_sb", [P, TT, 2 * HEADS, HD + 1], stack=mixer)
        hT = sb("hT", [P, KT, 2 * SEQ], F32R, stack=mixer)
        start = ExitStack()
        h0 = sb("h0", [P, TT, D], stack=start)
        sel = sb("sel", [HEADS, HEADS, P], stack=start)
        sel_r = sb("sel_r", [HEADS, HEADS, P], F32R, stack=start)
        neg_m = sb("neg_m", [HEADS, 2, SEQ], F32R, stack=start)
        rel = sb("rel", [P, 3 * P], stack=start)
        wg = sb("wg", [P, KT, 64], stack=start)
        wg_both = sb("wg_both", [P, KT, 104], F32R, stack=start)
        start.close()
        mixT = sb("mixT", [P, KT, 2 * SEQ], F32R, stack=mixer)
        qT = sb("qT", [P, 4, SEQ], stack=mixer)
        kT = sb("kT", [P, 4, SEQ], stack=mixer)
        gT = sb("gT", [P, 4, SEQ], stack=mixer)
        probs = sb("probs", [P, 3 * P], stack=mixer)
        y = sb("y", [P, 2, TT, HD], stack=mixer)
        pre = sb("pre", [P, 2, SEQ + CONV - 1], stack=mixer)
        cosT = sb("cosT", [P, SEQ], stack=mixer)
        sinT = sb("sinT", [P, SEQ], stack=mixer)
        a_col = sb("a_col", [P, TT, HEADS], stack=mixer)
        floor = sb("floor", [P, TT, 2 * HEADS], stack=mixer)
        vec = sb("vec", [P, 4], stack=mixer)
        mixer.close()
        new = pre[:, :, CONV - 1:]
        spin = gT[:, 0:2, :]
        ffn = ExitStack()
        ffT = sb("ffT", [P, KF, 2 * SEQ], F32R, stack=ffn)
        last = ExitStack()
        ff_out = sb("ff_out", [P, TT, D], stack=last)
        g_post2 = sb("g_post2", [P, D], stack=last)
        last.close()
        h2T = sb("h2T", [P, KT, 2 * SEQ], F32R, stack=ffn)
        ff_g = sb("ff_g", [P, 2, SEQ], stack=ffn)
        ff_u = sb("ff_u", [P, 2, SEQ], stack=ffn)
        ctx.callback(ffn.close)

        def row(n):
            return h0[:, n // 8, (n % 8) * SEQ:(n % 8 + 1) * SEQ]

        R_RIGHT, R_Z, R_ABS, R_EXP, R_LN, R_A, R_F, R_M, R_NEGM, R_NEGROW, R_ONES,\
            R_LEFT_LO, R_RIGHT_LO = range(13)

        bank = ctx.enter_context(nc.psum_tensor("bank", [P, 8, 512], F32))
        B_S, B_PV, B_T = 4, 5, 7

        def acc(pair):
            return bank[:, 2 * pair:2 * pair + 2, :]

        def spread(h):
            return bank[:, 4 + h // 2, (h % 2) * SEQ:(h % 2 + 1) * SEQ]

        def pv_out(a):
            return bank[:, B_PV + a % 2, 0:TT * (HD + 1)].rearrange("p (t c) -> p t c", t=TT)

        raw_full = [sem(f"raw_full{n}") for n in range(RAW_CHUNKS)]
        hi_done = sem("hi_done")
        lo_done = sem("lo_done")
        sub_done = sem("sub_done")
        acc_free = sem("acc_free")
        right_ready = sem("right_ready")
        x_in = [sem(f"x_in{t}") for t in range(TT)]
        small_in = sem("small_in")
        wg_in = sem("wg_in")
        post_in = sem("post_in")
        zeroed = sem("zeroed")
        consts = sem("consts")
        dve_step = sem("dve_step")
        sq_done = sem("sq_done")
        var_ready = sem("var_ready")
        sd_ready = sem("sd_ready")
        resid_ready = sem("resid_ready")
        h_ready = sem("h_ready")
        xT_done = sem("xT_done")
        xT_hi = sem("xT_hi")
        xT_lo = sem("xT_lo")
        coef_T = sem("coef_T")
        coef_ready = sem("coef_ready")
        wg_rounded = sem("wg_rounded")
        wg_ready = sem("wg_ready")
        gates_full = sem("gates_full")
        gates_act = sem("gates_act")
        gates_dve = sem("gates_dve")
        cols_T = sem("cols_T")
        cols_ready = sem("cols_ready")
        spread_done = sem("spread_done")
        masked = sem("masked")
        decay_ready = sem("decay_ready")
        angles = sem("angles")
        rope_ready = sem("rope_ready")
        tiles_done = sem("tiles_done")
        pair_ready = sem("pair_ready")
        gate_sig = sem("gate_sig")
        scores_done = sem("scores_done")
        probs_ready = sem("probs_ready")
        pv_done = sem("pv_done")
        den_ready = sem("den_ready")
        recip_ready = sem("recip_ready")
        y_ready = sem("y_ready")
        tile_full = sem("tile_full")
        yT_done = sem("yT_done")
        mix_ready = sem("mix_ready")
        mix_hi = sem("mix_hi")
        mix_lo = sem("mix_lo")
        gate_normed = sem("gate_normed")
        silu_done = sem("silu_done")
        gate_scaled = sem("gate_scaled")
        rms_spread = sem("rms_spread")
        ff_ready = sem("ff_ready")
        ff_hi = sem("ff_hi")
        ff_lo = sem("ff_lo")
        stored = sem("stored")

        SMALL = 16 * 10
        CONSTS = 8
        V_HEADS = TT
        V_POST1 = V_HEADS + 2 * HEADS + 1
        V_NORM2 = V_POST1 + TT
        V_POST2 = V_NORM2 + 1
        Q_HEADS = TT
        Q_POST1 = Q_HEADS + TT * 2 * HEADS
        Q_NORM2 = Q_POST1 + 4 * TT
        Q_POST2 = Q_NORM2 + TT
        CHUNKS = 4
        OUT_PARTS = 4

        def pair_of(group, part, u):
            return 4 * group + 2 * part + u

        block = ctx.enter_context(nc.Block())

        @block.sync
        def _(sp):
            def load(rnd, q, src, wait=True):
                if wait:
                    sp.wait_ge(lo_done, 8 * (rnd - 1) + 2 * q + 2)
                k = src.shape[1]
                sp.dma_start(raw[:, q, :].rearrange("p (k c) -> p k c", k=k), src)\
                  .then_inc(raw_full[q], 16)

            def rows(w, k0, n, col, width):
                return w[k0 * P:(k0 + n) * P, bass.ds(col, width)].rearrange("(k p) c -> p k c", p=P)

            for t in range(TT):
                sp.dma_start(resid[:, t, :], x[0, t * P:(t + 1) * P, :]).then_inc(x_in[t], 16)
            for src, r0, n in ((g_mix_pre, C_GPRE, 16), (g_ffn_pre, C_GFFN, 16),
                               (conv_b, C_CONVB, 16), (g_mlstm_head, C_GHEAD, 8),
                               (g_ret_head, C_GHEAD + 8, 8)):
                sp.dma_start(right[r0:r0 + n, 0, 0:P], src[0, :].rearrange("(r c) -> r c", c=P))\
                  .then_inc(small_in, 16)
            sp.dma_start(right[C_CONVW:C_CONVW + 64, 0, 0:P],
                         conv_w[0].rearrange("j (r c) -> (j r) c", c=P)).then_inc(small_in, 16)
            sp.dma_start(vec[0:HEADS, 2:3], b_igate[0, :].rearrange("(h o) -> h o", o=1))\
              .then_inc(small_in, 16)
            sp.dma_start(vec[32:32 + HEADS, 2:3], b_fgate[0, :].rearrange("(h o) -> h o", o=1))\
              .then_inc(small_in, 16)
            sp.dma_start(vec[:, 0:1], inv_freq).then_inc(small_in, 16)
            sp.dma_start(cosT[:].bitcast(I32), positions[0:1, :].partition_broadcast(P))\
              .then_inc(small_in, 16)
            for r in range(4):
                for q in range(4):
                    col = 2 * DH + (r % 2) * 512 + (r // 2) * COL_RET
                    load(r, q, rows(w_in, 4 * q, 4, col, 512), wait=r > 0)
            with sp.Fori(0, 2) as kind:
                with sp.Fori(0, 2) as half:
                    for n, part in enumerate((0, 1, 3)):
                        for q in range(4):
                            col = COL_RET * kind + 512 * half + (part * DH + (q // 2) * 256)
                            load(6 * kind + 3 * half + (R_IN + n), q,
                                 rows(w_in, 8 * (q % 2), 8, col, 256))
            with sp.Fori(0, 4) as g:
                for q in range(4):
                    load(g + R_OUT, q, rows(w_out, 4 * q, 4, 512 * g, 512))
            with sp.Fori(0, PAIRS) as i:
                for q in range(4):
                    load(i + R_FF, q, rows(w_gate if q < 2 else w_up, 8 * (q % 2), 8, 256 * i, 256))
            for n in range(4 * KF // 4):
                g, k = divmod(n, KF // 4)
                load(R_DOWN + n // 4, n % 4, rows(w_down, 4 * k, 4, 512 * g, 512))
            for t in range(TT):
                for c in range(OUT_PARTS):
                    sp.wait_ge(resid_ready, TT * CHUNKS + OUT_PARTS * t + c + 1)
                    cols = slice(c * D // OUT_PARTS, (c + 1) * D // OUT_PARTS)
                    sp.dma_start(out[0, t * P:(t + 1) * P, cols], resid[:, t, cols]).then_inc(stored, 16)
            sp.wait_ge(stored, 16 * TT * OUT_PARTS)

        @block.gpsimd
        def _(pool):
            pool.memset(ident, 0.0).then_inc(zeroed, 1)
            pool.memset(wg[:], 0.0).then_inc(zeroed, 1)
            pool.memset(sel[:], 0.0).then_inc(zeroed, 1)
            pool.iota(rel[:, 0:2 * P], [[1, 2 * P]], base=0, channel_multiplier=-1,
                      allow_small_or_imprecise_dtypes=True).then_inc(zeroed, 1)
            pool.iota(rel[:, 2 * P:3 * P], [[1, P]], base=0, channel_multiplier=-1,
                      allow_small_or_imprecise_dtypes=True).then_inc(zeroed, 1)
            pool.wait_ge(zeroed, 5)
            pool.affine_select(ident, ident, [[-1, P]], ALU.not_equal, 1.0, base=0,
                               channel_multiplier=1).then_inc(consts, 1)
            pool.affine_select(sel[:], sel[:], [[-1, HEADS], [0, P]], ALU.not_equal, 1.0, base=0,
                               channel_multiplier=1).then_inc(consts, 1)
            for c in (0, 2):
                pool.affine_select(rel[:, c * P:(c + 1) * P], rel[:, c * P:(c + 1) * P], [[1, P]],
                                   ALU.is_ge, 1e9, base=0, channel_multiplier=-1).then_inc(consts, 1)
            pool.memset(pre[:, :, 0:CONV - 1], 0.0).then_inc(consts, 1)
            pool.memset(v_sb[:, :, 0:HEADS, HD:HD + 1], 1.0).then_inc(consts, 1)
            pool.memset(v_sb[:, :, HEADS:2 * HEADS, HD:HD + 1], 0.0).then_inc(consts, 1)
            pool.memset(floor[:, :, HEADS:2 * HEADS], 1.0).then_inc(consts, 1)
            pool.dma_start(wg[:, :, 0:HEADS], w_in[:, 4 * DH:4 * DH + HEADS].rearrange(
                "(k p) c -> p k c", p=P)).then_inc(wg_in, 16)
            pool.dma_start(wg[:, :, 32:32 + HEADS], w_in[:, 4 * DH + HEADS:COL_RET].rearrange(
                "(k p) c -> p k c", p=P)).then_inc(wg_in, 16)
            for h in range(HEADS):
                pool.wait_ge(decay_ready, HEADS + h + 1)
                for c in (0, 2):
                    block_ = decay[:, h, c * P:(c + 1) * P]
                    ins = pool.affine_select(block_, block_, [[1, P]], ALU.is_ge, 0.0, base=0,
                                             channel_multiplier=-1)
                ins.then_inc(masked, 1)
            pool.wait_ge(probs_ready, 2 * HEADS)
            pool.dma_start(g_post1[:], g_mix_post[0:1, :].partition_broadcast(P)).then_inc(post_in, 16)
            pool.wait_ge(sub_done, 8 * R_DOWN)
            pool.dma_start(g_post2[:], g_ffn_post[0:1, :].partition_broadcast(P)).then_inc(post_in, 16)

        @block.scalar
        def _(act):
            def square_root_table():
                act.activation(stat[:, S_SPARE + 1:S_SPARE + 2], stat[:, S_SPARE:S_SPARE + 1], ACT.Sqrt)

            def hi(rnd, s):
                rnd, s = rnd + s // 8, s % 8
                act.wait_ge(raw_full[s // 2], 16 * (rnd + 1))
                act.activation(w_hi[:, s % AHEAD, :], raw[:, s // 2, (s % 2) * SUB:(s % 2 + 1) * SUB],
                               ACT.Copy).then_inc(hi_done, 1)

            def ahead(rnd, s):
                act.wait_ge(sub_done, 8 * rnd + s + 1)
                hi(rnd, s + AHEAD)

            def root(dst, src, count):
                act.wait_ge(var_ready, count)
                act.activation(dst, src, ACT.Sqrt).then_inc(sd_ready, 1)

            def transposed_hi(dst, gain, banks0, tiles=range(KT)):
                for k in tiles:
                    act.wait_ge(xT_done, banks0 + k // 2 + 1)
                    act.activation(dst[:, k, 0:SEQ], bank[:, k // 2, (k % 2) * SEQ:(k % 2 + 1) * SEQ],
                                   ACT.Copy, scale=coef[:, gain + k:gain + k + 1]).then_inc(xT_hi, 1)

            act.wait_ge(acc_free, 2)
            square_root_table()
            for t in range(TT):
                act.wait_ge(x_in[t], 16)
                act.activation(h0[:, t, :], resid[:, t, :], ACT.Square,
                               accum_out=stat[:, S_SQ + t:S_SQ + t + 1]).then_inc(sq_done, 1)
                root(stat[:, S_SD + t:S_SD + t + 1], stat[:, S_VAR + t:S_VAR + t + 1], t + 1)
            act.wait_ge(coef_ready, 1)
            for s in range(AHEAD):
                transposed_hi(hT, C_GPRE, 0, start_tiles(s))
                hi(0, s)
            transposed_hi(hT, C_GPRE, 0, start_tiles(AHEAD))

            def v_round(r, first=False):
                for s in range(8):
                    ahead(r, s)
                    if first and s == 0:
                        act.wait_ge(wg_in, 32)
                        act.activation(wg_both[:, :, 0:64], wg[:], ACT.Copy).then_inc(wg_rounded, 1)
                    if first and s == 7:
                        act.activation(sel_r[:], sel[:], ACT.Copy)
                    if first and s in (4, 6):
                        n = s // 2 - 2
                        act.wait_ge(angles, n + 1)
                        act.activation((sinT, cosT)[n][:], row(2 + n), ACT.Sin,
                                       scale=1.0 if n else vec[:, 1:2]).then_inc(rope_ready, 1)
                    if first and s >= 6:
                        act.wait_ge(consts, CONSTS)
                        for h in range(4 * s - 24, 4 * s - 20):
                            act.activation(decay[:, HEADS + h, :], rel[:], ACT.Exp, scale=LOG_GAMMA[h])\
                               .then_inc(decay_ready, 1)

            v_round(0, first=True)
            with act.Fori(1, 4) as r:
                v_round(r)

            def mlstm_decay(h):
                if h == 0:
                    act.wait_ge(cols_ready, 1)
                    act.activation(floor[:, :, 0:HEADS], floor[:, :, 0:HEADS], ACT.Exp)
                if h % 2 == 0:
                    act.wait_ge(spread_done, h + 2)
                act.activation(decay[:, h, 0:SEQ], spread(h), ACT.Exp, bias=a_col[:, 0, h:h + 1])
                act.activation(decay[:, h, SEQ:3 * P], spread(h)[:, P:2 * P], ACT.Exp,
                               bias=a_col[:, 1, h:h + 1]).then_inc(decay_ready, 1)

            def copy_right(pair, event):
                act.wait_ge(acc_free, event + 2)
                act.activation(right[:], acc(pair)[:, :, SEQ:2 * SEQ], ACT.Copy)\
                   .then_inc(right_ready, 1)

            def head_col(a, c):
                return S_HEAD + S_HEAD_COLS * (a % 2) + c

            def head_stat(a, c):
                return stat[:, head_col(a, c):head_col(a, c) + 2]

            def head_step(rnd, s):
                a = head_at(rnd, s, 4)
                if a is not None:
                    root(head_stat(a, H_SD), head_stat(a, H_VAR), V_HEADS + a + 1)
                a = head_at(rnd, s, 3)
                if a is not None:
                    act.wait_ge(recip_ready, a + 1)
                    for t in range(TT):
                        if t:
                            act.wait_ge(sq_done, Q_HEADS + TT * a + t)
                        r, q = head_col(a, H_RECIP) + t, head_col(a, H_SQ) + t
                        act.activation(bank[:, B_PV + a % 2, 384:512], pv_out(a)[:, t, 0:HD],
                                       ACT.Square, scale=stat[:, r:r + 1],
                                       accum_out=stat[:, q:q + 1]).then_inc(sq_done, 1)
                a = head_at(rnd, s, 2)
                if a is not None:
                    act.wait_ge(pv_done, a + 1)
                    act.activation(head_stat(a, H_DEN), pv_out(a)[:, :, HD], ACT.Abs).then_inc(den_ready, 1)
                a = head_at(rnd, s, 7)
                if a is not None:
                    act.wait_ge(mix_ready, a + 1)
                    act.activation(mixT[:, a, 0:SEQ], gT[:, a % 4, :], ACT.Copy).then_inc(mix_hi, 1)

            def mixer_step(rnd, s):
                ended = unit_at(rnd, s, 0)
                if ended:
                    copy_right(ended[2], event_of(rnd, ended[2]))
                ended = unit_at(rnd, s, 1)
                if ended and ended[1] == 2:
                    group, part, u = ended
                    two = slice(2 * u, 2 * u + 2)
                    act.wait_ge(acc_free, event_of(gate_round(group), u) + 3)
                    act.activation(new if group >= 2 else gT[:, two, :], gT[:, two, :], ACT.Sigmoid)\
                       .then_inc(gate_sig, 1)
                ended = unit_at(rnd, s, 2)
                if ended and ended[1] < 2:
                    group, part, u = ended
                    act.wait_ge(tiles_done, pair_of(group, part, u) + 1)
                    act.activation((qT, kT)[part][:, 2 * u:2 * u + 2, :], new,
                                   ACT.Silu if group < 2 else ACT.Copy).then_inc(pair_ready, 1)

            def gate_rows():
                act.wait_ge(gates_full, 1)
                act.activation(row(R_RIGHT)[0:40], bank[0:40, 5, SEQ:2 * SEQ], ACT.Copy)
                act.activation(row(R_LEFT_LO)[0:40], bank[64:104, 5, 0:SEQ], ACT.Copy)
                act.activation(row(R_RIGHT_LO)[0:40], bank[64:104, 5, SEQ:2 * SEQ], ACT.Copy)\
                   .then_inc(gates_act, 1)
                act.wait_ge(gates_dve, 3)
                act.activation(row(R_EXP)[32:40], row(R_ABS)[32:40], ACT.Exp, scale=-1.0)\
                   .then_inc(gates_act, 1)
                act.wait_ge(gates_act, 2)
                act.activation(row(R_LN)[32:40], row(R_EXP)[32:40], ACT.Ln, bias=1.0)\
                   .then_inc(gates_act, 1)

            def gate_rows_rest():
                act.wait_ge(gates_dve, 9)
                act.activation(neg_m[:, 0, :], row(R_NEGM)[0:HEADS], ACT.Copy).then_inc(gates_act, 1)

            gate_rows()
            for rnd in range(R_IN, R_OUT):
                for s in range(8):
                    head_step(rnd, s)
                    ahead(rnd, s)
                    mixer_step(rnd, s)
                    if rnd == R_IN and s == 1:
                        gate_rows_rest()
                    if rnd == R_IN + 1 and 2 <= s < 5:
                        for h in range(3 * s - 6, min(3 * s - 3, HEADS)):
                            mlstm_decay(h)

            def squares(pair, g, t, count):
                act.wait_ge(sq_done, count + TT * g + t)
                act.activation(bank[:, B_S, :], acc(pair)[:, t, :], ACT.Square,
                               accum_out=stat[:, S_PSQ + 4 * t + g:S_PSQ + 4 * t + g + 1])\
                   .then_inc(sq_done, 1)

            def last_squares(t, subs, results, count, roots):
                if t == 0:
                    act.wait_ge(tile_full, results)
                else:
                    act.wait_ge(sub_done, subs)
                squares(1, 3, t, count)
                root(stat[:, S_PSD + t:S_PSD + t + 1], stat[:, S_PVAR + t:S_PVAR + t + 1], roots + t)

            for rnd in range(R_OUT, R_FF - 1):
                for s in range(8):
                    head_step(rnd, s)
                    ahead(rnd, s)
                    mixer_step(rnd, s)
                if rnd == R_OUT:
                    square_root_table()
                for t in range(TT):
                    squares(rnd % 2, rnd - R_OUT, t, Q_POST1)
            for s in range(8 - SPLIT_OUT):
                ahead(R_FF - 1, s)
            last_squares(0, 8 * R_FF, 1, Q_POST1, V_POST1)
            for s in range(8 - SPLIT_OUT, 7):
                ahead(R_FF - 1, s)
            last_squares(1, 8 * R_FF, 1, Q_POST1, V_POST1)
            ahead(R_FF - 1, 7)

            for c in range(CHUNKS):
                transposed_hi(h2T, C_GFFN, KT // 2, range(4 * c, 4 * c + 4))

            def ffn_pair(i, first=False):
                for s in range(8):
                    ahead(i + R_FF, s)
                    if first and s < TT:
                        act.wait_ge(resid_ready, TT * CHUNKS)
                        act.activation(mixed[:, s, :], resid[:, s, :], ACT.Square,
                                       accum_out=stat[:, S_SQ + s:S_SQ + s + 1]).then_inc(sq_done, 1)
                    if first and s == 2:
                        root(stat[:, S_SD:S_SD + 2], stat[:, S_VAR:S_VAR + 2], V_NORM2)
                    if s == 3:
                        copy_right(0, 2 * i + E_FF)
                    if s == (6 if first else 4):
                        act.wait_ge(gate_normed, i + 1)
                        act.activation(ff_g[:], ff_g[:], ACT.Silu).then_inc(silu_done, 1)
                    if s == 7:
                        copy_right(1, 2 * i + (E_FF + 1))
                        act.wait_ge(ff_ready, i + 1)
                        act.activation(ffT[:, bass.ds(2 * i, 2), 0:SEQ], ff_u[:], ACT.Copy)\
                           .then_inc(ff_hi, 1)

            ffn_pair(0, first=True)
            with act.Fori(1, PAIRS) as i:
                ffn_pair(i)

            square_root_table()
            for g in range(4):
                full, end = divmod(DOWN_SUBS * (g + 1) - 1, 8)
                with act.Fori(3 * g, full) as r:
                    for s in range(8):
                        ahead(r + R_DOWN, s)
                for s in range(8 if g < 3 else 8 - AHEAD):
                    ahead(R_DOWN + full, s)
                    if s == end:
                        for t in range(TT):
                            squares(g % 2, g, t, Q_POST2)
            for t in range(TT):
                last_squares(t, N_SUBS, 2, Q_POST2, V_POST2)

        @block.vector
        def _(dve):
            steps = [0]

            def link(ins):
                steps[0] += 1
                ins.then_inc(dve_step, 1)
                dve.wait_ge(dve_step, steps[0])

            def lo(rnd, s):
                rnd, s = rnd + s // 8, s % 8
                dve.wait_ge(hi_done, 8 * rnd + s + 1)
                dve.tensor_tensor(w_lo[:, s % AHEAD, :], raw[:, s // 2, (s % 2) * SUB:(s % 2 + 1) * SUB],
                                  w_hi[:, s % AHEAD, :].bitcast(F32), ALU.subtract).then_inc(lo_done, 1)

            def transposed_lo(dst, gain, tiles0, tiles=range(KT)):
                for k in tiles:
                    dve.wait_ge(xT_hi, tiles0 + 2 * (k // 2) + 2)
                    dve.scalar_tensor_tensor(
                        dst[:, k, SEQ:2 * SEQ], bank[:, k // 2, (k % 2) * SEQ:(k % 2 + 1) * SEQ],
                        coef[:, gain + k:gain + k + 1], dst[:, k, 0:SEQ].bitcast(F32),
                        ALU.mult, ALU.subtract).then_inc(xT_lo, 1)

            dve.memset(vec[0:64, 1:2], 1.0)
            dve.memset(vec[64:128, 1:2], -1.0)
            dve.memset(stat[:, S_SPARE:S_SPARE + 1], 0.0).then_inc(acc_free, 2)
            dve.memset(stat[:, S_SPARE + 2:S_SPARE + 3], 0.0).then_inc(y_ready, 2)
            for t in range(TT):
                dve.wait_ge(sq_done, t + 1)
                dve.tensor_scalar(stat[:, S_VAR + t:S_VAR + t + 1], stat[:, S_SQ + t:S_SQ + t + 1],
                                  1.0 / D, EPS, ALU.mult, ALU.add).then_inc(var_ready, 1)
                dve.wait_ge(sd_ready, t + 1)
                link(dve.reciprocal(stat[:, S_RSTD + t:S_RSTD + t + 1], stat[:, S_SD + t:S_SD + t + 1]))
                for c in range(CHUNKS):
                    cols = slice(512 * c, 512 * (c + 1))
                    dve.tensor_scalar(h0[:, t, cols], resid[:, t, cols],
                                      stat[:, S_RSTD + t:S_RSTD + t + 1], None, ALU.mult)\
                       .then_inc(h_ready, 1)
                if t == 0:
                    dve.wait_ge(coef_T, 1)
                    dve.tensor_copy(coef, bank[:, 7, 0:P]).then_inc(coef_ready, 1)
            dve.wait_ge(coef_ready, 1)
            for s in range(AHEAD):
                transposed_lo(hT, C_GPRE, 0, start_tiles(s))
                lo(0, s)
            transposed_lo(hT, C_GPRE, 0, start_tiles(AHEAD))

            pos, ang, turns = row(0), row(1), row(4)

            def angle(dst, quarter):
                link(dve.tensor_scalar(turns, ang, 1.0 / (2 * math.pi), quarter, ALU.mult, ALU.add))
                link(dve.tensor_scalar(turns, turns, ROUND, None, ALU.add))
                link(dve.tensor_scalar(turns, turns, ROUND, quarter, ALU.subtract, ALU.subtract))
                link(dve.scalar_tensor_tensor(dst, turns, -TWO_PI_1, ang, ALU.mult, ALU.add))
                link(dve.scalar_tensor_tensor(dst, turns, -TWO_PI_2, dst, ALU.mult, ALU.add))
                link(dve.scalar_tensor_tensor(dst, turns, -TWO_PI_3, dst, ALU.mult, ALU.add))
                dve.tensor_scalar(dst, dst, -3.1415925, 3.1415925, ALU.max, ALU.min).then_inc(angles, 1)

            def v_rounds(i, first=False):
                for e in range(2):
                    for s in range(8):
                        lo(2 * i + e, s + AHEAD)
                        if first and e == 0 and s == 2:
                            dve.wait_ge(small_in, SMALL)
                            link(dve.tensor_copy(pos, cosT[:].bitcast(I32)))
                            link(dve.tensor_scalar(ang, pos, vec[:, 0:1], None, ALU.mult))
                            angle(row(2), 0.0)
                        if first and e == 0 and s == 4:
                            angle(row(3), 0.25)
                        if first and e == 0 and s == 5:
                            dve.wait_ge(wg_rounded, 1)
                            dve.tensor_tensor(wg_both[:, :, 64:104], wg[:, :, 0:40],
                                              wg_both[:, :, 0:40].bitcast(F32), ALU.subtract)\
                               .then_inc(wg_ready, 1)
                    dve.wait_ge(sub_done, 16 * i + (8 * e + 8))
                    for t in range(TT):
                        ins = dve.tensor_copy(v_sb[:, t, bass.ds(8 * i + 4 * e, 4), 0:HD],
                                              acc(e)[:, t, :].rearrange("p (h c) -> p h c", c=HD))
                    ins.then_inc(acc_free, 1)

            v_rounds(0, first=True)
            v_rounds(1)

            def gates(ins, n):
                ins.then_inc(gates_dve, 1)
                dve.wait_ge(gates_dve, n)

            def rowi(n):
                return row(n)[0:HEADS]

            def rowf(n):
                return row(n)[32:32 + HEADS]

            dve.wait_ge(rope_ready, 2)
            dve.wait_ge(gates_act, 1)
            for n, p0 in enumerate((0, 32)):
                z = row(R_Z)[p0:p0 + HEADS]
                link(dve.scalar_tensor_tensor(z, row(R_LEFT_LO)[p0:p0 + HEADS], 1.0,
                                              row(R_RIGHT_LO)[p0:p0 + HEADS], ALU.mult, ALU.add))
                link(dve.tensor_tensor(z, z, row(R_RIGHT)[p0:p0 + HEADS], ALU.add))
                gates(dve.scalar_tensor_tensor(z, bank[p0:p0 + HEADS, 5, 0:SEQ],
                                               vec[p0:p0 + HEADS, 2:3], z, ALU.add, ALU.add), n + 1)
            gates(dve.scalar_tensor_tensor(rowf(R_ABS), rowf(R_Z), -1.0, rowf(R_Z), ALU.mult, ALU.max), 3)
            link(dve.memset(rowf(R_ONES), 1.0))
            dve.wait_ge(gates_act, 3)
            gates(dve.scalar_tensor_tensor(rowf(R_A), rowf(R_Z), 0.0, rowf(R_LN), ALU.min, ALU.subtract), 4)
            gates(dve.tensor_tensor_scan(rowf(R_F), rowf(R_ONES), rowf(R_A), 0.0, ALU.mult, ALU.add), 5)

            def gate_rows_rest():
                gates(dve.tensor_copy(rowi(R_F), rowf(R_F)), 6)
                gates(dve.tensor_tensor(rowi(R_A), rowi(R_Z), rowi(R_F), ALU.subtract), 7)
                gates(dve.tensor_tensor_scan(rowi(R_M), rowi(R_A), rowi(R_A), 0.0, ALU.max, ALU.max), 8)
                gates(dve.tensor_scalar(rowi(R_NEGM), rowi(R_M), -1.0, None, ALU.mult), 9)
                gates(dve.scalar_tensor_tensor(rowi(R_NEGROW), rowi(R_F), -1.0, rowi(R_M), ALU.mult,
                                               ALU.subtract), 10)
                dve.wait_ge(gates_act, 4)
                dve.tensor_tensor(neg_m[:, 1, :], rowi(R_NEGM), neg_m[:, 0, :].bitcast(F32),
                                  ALU.subtract).then_inc(gates_dve, 1)

            def gate_columns():
                dve.wait_ge(cols_T, 1)
                cols = bank[:, 4, 0:4 * HEADS].rearrange("p (n t h) -> p n t h", n=2, t=TT)
                dve.tensor_copy(a_col[:], cols[:, 0])
                dve.wait_ge(consts, CONSTS)
                dve.tensor_copy(floor[:, :, 0:HEADS], cols[:, 1]).then_inc(cols_ready, 1)

            def unit_sums(rnd, u, part):
                event = event_of(rnd, u)
                dve.wait_ge(right_ready, event - E_IN + 1)
                summed = gT[:, 2 * u:2 * u + 2, :] if part == 2 else new
                dve.tensor_tensor(summed, acc(u)[:, :, 0:SEQ], right[:], ALU.add).then_inc(acc_free, 1)
                dve.wait_ge(acc_free, event + 3)

            def signalled(ins):
                steps[0] += 1
                ins.then_inc(dve_step, 1)
                return steps[0]

            conv_step = [0, 0]

            def convolve(group, part, u, half):
                for j in (2 * half, 2 * half + 1):
                    for c in range(2):
                        n = HEADS * part + 4 * group + 2 * u + c
                        tap = coef[:, C_CONVW + 16 * j + n:C_CONVW + 16 * j + n + 1]
                        src, work = pre[:, c, j:j + SEQ], spin[:, c, :]
                        if j == 0:
                            ins = dve.tensor_scalar(work, src, tap, coef[:, C_CONVB + n:C_CONVB + n + 1],
                                                    ALU.mult, ALU.add)
                        else:
                            dve.wait_ge(dve_step, conv_step[c])
                            ins = dve.scalar_tensor_tensor(work if j < CONV - 1 else new[:, c, :], src,
                                                           tap, work, ALU.mult, ALU.add)
                        conv_step[c] = signalled(ins) if j < CONV - 1 else 0
                if half:
                    ins.then_inc(tiles_done, 1)

            def rotate(group, part, u, half):
                if half == 0:
                    for p0, p1 in ((0, 64), (64, 0)):
                        ins = dve.tensor_tensor(spin[p0:p0 + 64], new[p1:p1 + 64],
                                                two(sinT[p1:p1 + 64, :], 64), ALU.mult)
                    link(ins)
                    conv_step[0] = signalled(dve.tensor_tensor(new, new, two(cosT[:], P), ALU.mult))
                else:
                    dve.wait_ge(dve_step, conv_step[0])
                    dve.tensor_tensor(new, new, spin, ALU.add).then_inc(tiles_done, 1)

            def two(table, rows):
                return table.unsqueeze(1).to_broadcast([rows, 2, SEQ])

            def weigh(a):
                dve.wait_ge(scores_done, a + 1)
                dve.wait_ge(*((masked, a + 1) if a < HEADS else (decay_ready, HEADS)))
                if a >= 1:
                    dve.wait_ge(pv_done, a)
                dve.scalar_tensor_tensor(probs[:], bank[:, B_S, 0:3 * P], SCALE, decay[:, a, :],
                                         ALU.mult, ALU.mult).then_inc(probs_ready, 1)

            def head_stat(a, c):
                c += S_HEAD + S_HEAD_COLS * (a % 2)
                return stat[:, c:c + 2]

            def head_recip(a):
                dve.wait_ge(den_ready, a + 1)
                link(dve.tensor_tensor(head_stat(a, H_DEN), head_stat(a, H_DEN), floor[:, :, a], ALU.max))
                dve.reciprocal(head_stat(a, H_RECIP), head_stat(a, H_DEN)).then_inc(recip_ready, 1)

            def head_variance(a):
                dve.wait_ge(sq_done, Q_HEADS + TT * (a + 1))
                dve.tensor_scalar(head_stat(a, H_VAR), head_stat(a, H_SQ), 1.0 / HD, EPS, ALU.mult,
                                  ALU.add).then_inc(var_ready, 1)

            def head_scaled(a):
                dve.wait_ge(sd_ready, V_HEADS + a + 1)
                link(dve.reciprocal(head_stat(a, H_RSTD), head_stat(a, H_SD)))
                link(dve.tensor_tensor(head_stat(a, H_SCALE), head_stat(a, H_RSTD),
                                       head_stat(a, H_RECIP), ALU.mult))
                if a >= 2:
                    dve.wait_ge(yT_done, a - 1)
                for t in range(TT):
                    ins = dve.tensor_scalar(y[:, a % 2, t, :], pv_out(a)[:, t, 0:HD],
                                            head_stat(a, H_SCALE)[:, t:t + 1], None, ALU.mult)
                ins.then_inc(y_ready, 1)

            def mix(a):
                dve.wait_ge(yT_done, a + 1)
                dve.wait_ge(gate_sig, a // 2 + 1)
                dve.scalar_tensor_tensor(gT[:, a % 4, :], bank[:, B_T, 0:SEQ],
                                         coef[:, C_GHEAD + a:C_GHEAD + a + 1], gT[:, a % 4, :],
                                         ALU.mult, ALU.mult).then_inc(mix_ready, 1)

            def mix_rest(a):
                dve.wait_ge(mix_hi, a + 1)
                dve.tensor_tensor(mixT[:, a, SEQ:2 * SEQ], gT[:, a % 4, :],
                                  mixT[:, a, 0:SEQ].bitcast(F32), ALU.subtract).then_inc(mix_lo, 1)

            def head_step(rnd, s):
                for step, first in ((weigh, 0), (mix, 6), (head_scaled, 4), (head_variance, 3),
                                    (head_recip, 2), (mix_rest, 8)):
                    a = head_at(rnd, s, first)
                    if a is not None:
                        step(a)

            def mixer_step(rnd, s):
                for half in (1, 0):
                    ended = unit_at(rnd, s, half)
                    if ended:
                        group, part, u = ended
                        if half == 0:
                            unit_sums(rnd, u, part)
                        if part < 2:
                            (convolve if group < 2 else rotate)(group, part, u, half)
                ended = unit_at(rnd, s, 2)
                if ended and ended[0] >= 2 and ended[1] == 2:
                    group, part, u = ended
                    dve.wait_ge(gate_sig, 2 * group + u + 1)
                    link(dve.tensor_tensor(gT[:, 2 * u:2 * u + 2, :], gT[:, 2 * u:2 * u + 2, :], new,
                                           ALU.mult))

            for rnd in range(R_IN, R_OUT):
                for s in range(8):
                    head_step(rnd, s)
                    lo(rnd, s + AHEAD)
                    mixer_step(rnd, s)
                    if rnd == R_IN and s == 1:
                        gate_rows_rest()
                    if rnd == R_IN and s == 6:
                        gate_columns()

            def emptied(pair, dst, gain, g, squares0):
                for t in range(TT):
                    dve.wait_ge(sq_done, squares0 + TT * g + t + 1)
                    ins = dve.tensor_tensor(dst[:, t, 512 * g:512 * (g + 1)], acc(pair)[:, t, :],
                                            gain[:, 512 * g:512 * (g + 1)], ALU.mult)
                ins.then_inc(acc_free, 1)

            def last_columns(dst, gain, squares0, t, sd_count):
                dve.wait_ge(sq_done, squares0 + TT * 3 + t + 1)
                link(dve.tensor_reduce(stat[:, S_PSUM + t:S_PSUM + t + 1],
                                       stat[:, S_PSQ + 4 * t:S_PSQ + 4 * t + 4],
                                       mybir.AxisListType.X, ALU.add))
                dve.tensor_scalar(stat[:, S_PVAR + t:S_PVAR + t + 1], stat[:, S_PSUM + t:S_PSUM + t + 1],
                                  1.0 / D, EPS, ALU.mult, ALU.add).then_inc(var_ready, 1)
                link(dve.tensor_tensor(dst[:, t, 3 * 512:D], acc(1)[:, t, :], gain[:, 3 * 512:D],
                                       ALU.mult))
                dve.wait_ge(sd_ready, sd_count + t)
                link(dve.reciprocal(stat[:, S_PRSTD + t:S_PRSTD + t + 1],
                                    stat[:, S_PSD + t:S_PSD + t + 1]))

            def add_result(src, t, c0, c1):
                dve.scalar_tensor_tensor(resid[:, t, c0:c1], src[:, t, c0:c1],
                                         stat[:, S_PRSTD + t:S_PRSTD + t + 1], resid[:, t, c0:c1],
                                         ALU.mult, ALU.add).then_inc(resid_ready, 1)

            for rnd in range(R_OUT, R_FF - 1):
                g = rnd - R_OUT
                for s in range(8):
                    head_step(rnd, s)
                    lo(rnd, s + AHEAD)
                    mixer_step(rnd, s)
                if g == 0:
                    dve.wait_ge(post_in, 16)
                emptied(rnd % 2, mixed, g_post1, g, Q_POST1)
            for s in range(8 - SPLIT_OUT):
                lo(R_FF - 1, s + AHEAD)
            dve.wait_ge(acc_free, E_FF + 1)
            last_columns(mixed, g_post1, Q_POST1, 0, V_POST1)
            for c in range(2):
                add_result(mixed, 0, 512 * c, 512 * (c + 1))
            last_columns(mixed, g_post1, Q_POST1, 1, V_POST1)
            dve.sem_inc(acc_free, 1)
            for c in range(CHUNKS + 1):
                if c < CHUNKS:
                    for t in range(0 if c >= 2 else 1, TT):
                        add_result(mixed, t, 512 * c, 512 * (c + 1))
                if c:
                    transposed_lo(h2T, C_GFFN, KT, range(4 * c - 4, 4 * c))
                if 1 <= c <= SPLIT_OUT:
                    lo(R_FF - 1, 7 - SPLIT_OUT + c + AHEAD)

            def token_norms_a():
                dve.wait_ge(sq_done, Q_NORM2 + TT)
                dve.tensor_scalar(stat[:, S_VAR:S_VAR + 2], stat[:, S_SQ:S_SQ + 2], 1.0 / D, EPS,
                                  ALU.mult, ALU.add).then_inc(var_ready, 1)
                dve.wait_ge(sd_ready, V_NORM2)
                link(dve.reciprocal(stat[:, S_RSTD:S_RSTD + 2], stat[:, S_SD:S_SD + 2]))
                for t in range(TT):
                    link(dve.memset(ff_u[:, 0, t * P:(t + 1) * P], 1.0))
                    dve.tensor_scalar(ff_u[:, 0, t * P:(t + 1) * P], ff_u[:, 0, t * P:(t + 1) * P],
                                      stat[:, S_RSTD + t:S_RSTD + t + 1], None, ALU.mult)\
                       .then_inc(h_ready, 1)

            def token_norms_b():
                dve.wait_ge(rms_spread, 1)
                link(dve.tensor_copy(rms_row, bank[:, B_S, 0:SEQ]))

            def ffn_pair(i, first=False):
                for s in range(8):
                    lo(i + R_FF, s + AHEAD)
                    if first and s == 2:
                        token_norms_a()
                    if s == 3:
                        dve.wait_ge(right_ready, 2 * i + (E_OUT - E_IN + 1))
                        dve.tensor_tensor(ff_g[:], acc(0)[:, :, 0:SEQ], right[:], ALU.add)\
                           .then_inc(acc_free, 1)
                    if first and s == 5:
                        token_norms_b()
                    if s == (5 if first else 3):
                        dve.wait_ge(acc_free, 2 * i + (E_FF + 3))
                        dve.tensor_tensor(ff_g[:], ff_g[:], rms2, ALU.mult).then_inc(gate_normed, 1)
                    if s == (7 if first else 5):
                        dve.wait_ge(silu_done, i + 1)
                        dve.tensor_tensor(ff_g[:], ff_g[:], rms2, ALU.mult).then_inc(gate_scaled, 1)
                    if s == 7:
                        dve.wait_ge(right_ready, 2 * i + (E_OUT - E_IN + 2))
                        dve.tensor_tensor(ff_u[:], acc(1)[:, :, 0:SEQ], right[:], ALU.add)\
                           .then_inc(acc_free, 1)
                        dve.wait_ge(acc_free, 2 * i + (E_FF + 4))
                        dve.wait_ge(gate_scaled, i + 1)
                        dve.tensor_tensor(ff_u[:], ff_u[:], ff_g[:], ALU.mult).then_inc(ff_ready, 1)
                        dve.wait_ge(ff_hi, i + 1)
                        dve.tensor_tensor(ffT[:, bass.ds(2 * i, 2), SEQ:2 * SEQ], ff_u[:],
                                          ffT[:, bass.ds(2 * i, 2), 0:SEQ].bitcast(F32), ALU.subtract)\
                           .then_inc(ff_lo, 1)

            rms2 = rms_row.unsqueeze(1).to_broadcast([P, 2, SEQ])
            ffn_pair(0, first=True)
            with dve.Fori(1, PAIRS) as i:
                ffn_pair(i)

            for g in range(4):
                full, end = divmod(DOWN_SUBS * (g + 1) - 1, 8)
                with dve.Fori(3 * g, full) as r:
                    for s in range(8):
                        lo(r + R_DOWN, s + AHEAD)
                for s in range(8 if g < 3 else 8 - AHEAD):
                    lo(R_DOWN + full, s + AHEAD)
                    if s == end:
                        if g == 0:
                            dve.wait_ge(post_in, 32)
                        emptied(g % 2, ff_out, g_post2, g, Q_POST2)
            dve.wait_ge(acc_free, E_DOWN + 4 + 1)
            for t in range(TT):
                last_columns(ff_out, g_post2, Q_POST2, t, V_POST2)
                for c in range(OUT_PARTS):
                    add_result(ff_out, t, c * D // OUT_PARTS, (c + 1) * D // OUT_PARTS)

        @block.tensor
        def _(pe):
            def mm(out_, lhsT, rhs, start, stop):
                return pe.matmul(out_, lhsT, rhs, start=start, stop=stop, skip_group_check=True)

            def transposed(src, t, b):
                for k in range(2):
                    ins = pe.transpose(bank[:, b, k * SEQ + t * P:k * SEQ + (t + 1) * P],
                                       src[:, t, (2 * b + k) * P:(2 * b + k + 1) * P], ident)
                if t == TT - 1:
                    ins.then_inc(xT_done, 1)

            def sub_columns(rnd, s, act_T, pair):
                pe.wait_ge(lo_done, 8 * rnd + s + 1)
                slot, quarter = s % AHEAD, s % 4
                for c in range(2):
                    for j in range(4):
                        k = 4 * quarter + j
                        cols = slice(256 * j + P * c, 256 * j + P * (c + 1))
                        mm(bank[:, 2 * pair + c, :], w_hi[:, slot, cols], act_T[:, k, :], k == 0, False)
                        ins = mm(bank[:, 2 * pair + c, 0:SEQ], w_lo[:, slot, cols], act_T[:, k, 0:SEQ],
                                 False, k == KT - 1)
                ins.then_inc(sub_done, 1)

            def unit_columns(rnd, unit, event, act_T, before=None, after=None):
                pe.wait_ge(acc_free, event + 1)
                for q in range(4):
                    s = 4 * unit + q
                    if before:
                        before(s)
                    sub_columns(rnd, s, act_T, unit)
                    if after:
                        after(s)

            def sub_tokens(count, slot, act_T, pair, k0, last, tiles=range(TT)):
                pe.wait_ge(lo_done, count)
                for j in range(2):
                    k, w = k0 + j, slice(512 * j, 512 * (j + 1))
                    for t in tiles:
                        hi_x = act_T[:, k, t * P:(t + 1) * P]
                        lo_x = act_T[:, k, SEQ + t * P:SEQ + (t + 1) * P]
                        mm(bank[:, 2 * pair + t, :], hi_x, w_hi[:, slot, w], k == 0, False)
                        mm(bank[:, 2 * pair + t, :], hi_x, w_lo[:, slot, w], False, False)
                        ins = mm(bank[:, 2 * pair + t, :], lo_x, w_hi[:, slot, w], False, k == last)
                if TT - 1 in tiles:
                    ins.then_inc(sub_done, 1)
                return ins

            def last_subs(rnd, first, subs, act_T, pair):
                for t in range(TT):
                    for s in range(first, subs):
                        ins = sub_tokens(rnd + s + 1, (rnd + s) % AHEAD, act_T, pair, 2 * s,
                                         2 * subs - 1, (t,))
                    if t == 0:
                        ins.then_inc(tile_full, 1)

            def keep_clock(products, b):
                for _ in range(products):
                    mm(bank[:, b, 0:P], ident, ident, True, True)

            pe.wait_ge(consts, 1)
            keep_clock(17, 6)
            pe.wait_ge(small_in, SMALL)
            pe.transpose(bank[:, 7, 0:P], right[:, 0, 0:P], ident).then_inc(coef_T, 1)
            def start_transposed(t, c):
                pe.wait_ge(h_ready, CHUNKS * t + c + 1)
                for b in (2 * c, 2 * c + 1):
                    transposed(h0, t, b)

            for c in range(CHUNKS - 1):
                start_transposed(0, c)
            pe.wait_ge(coef_ready, 1)
            keep_clock(2, 7)
            for c in range(CHUNKS - 1):
                start_transposed(1, c)
            keep_clock(6, 7)
            for t in range(TT):
                start_transposed(t, CHUNKS - 1)

            with pe.Fori(0, 2) as i:
                for e in range(2):
                    pe.wait_ge(acc_free, 2 * i + (e + 1))
                    for s in range(8):
                        pe.wait_ge(xT_lo, max(2 * s + 2, 4))
                        sub_tokens(16 * i + (8 * e + s + 1), s % AHEAD, hT, e, 2 * s, KT - 1)

            pe.wait_ge(wg_ready, 1)
            for k in range(KT):
                ins = mm(bank[0:104, 5, :], wg_both[:, k, :], hT[:, k, :], k == 0, k == KT - 1)
            ins.then_inc(gates_full, 1)

            def gate_columns():
                pe.wait_ge(gates_dve, 11)
                for n, r in enumerate((R_A, R_NEGROW)):
                    for t in range(TT):
                        c = (TT * n + t) * HEADS
                        ins = pe.transpose(bank[:, 4, c:c + HEADS], row(r)[0:HEADS, t * P:(t + 1) * P],
                                           ident[0:HEADS, 0:HEADS])
                ins.then_inc(cols_T, 1)

            def spread_rows():
                pe.wait_ge(consts, CONSTS)
                pe.wait_ge(cols_ready, 1)
                for h in range(HEADS):
                    mm(spread(h), sel_r[:, h, :], neg_m[:, 0, :], True, False)
                    mm(spread(h), sel_r[:, h, :], neg_m[:, 1, :], False, True).then_inc(spread_done, 1)

            def scores(group, n):
                pe.wait_ge(decay_ready, 2 * HEADS)
                pe.wait_ge(pair_ready, 4 * group + (3 + n // 2))
                mm(bank[:, B_S, 0:SEQ], kT[:, n, 0:P], qT[:, n, :], True, True)
                mm(bank[:, B_S, SEQ:SEQ + P], kT[:, n, P:2 * P], qT[:, n, P:2 * P], True, True)\
                    .then_inc(scores_done, 1)

            def weighted(group, n):
                pe.wait_ge(probs_ready, 4 * group + (n + 1))
                pe.wait_ge(y_ready, 4 * group + (n + 1))
                o = bank[:, B_PV + n % 2, :]
                v = v_sb[:, :, bass.ds(4 * group + n, 1), :].rearrange("p t o c -> p t (o c)")
                mm(o[:, 0:HD + 1], probs[:, 0:P], v[:, 0, :], True, True)
                mm(o[:, HD + 1:2 * (HD + 1)], probs[:, P:2 * P], v[:, 0, :], False, False)
                mm(o[:, HD + 1:2 * (HD + 1)], probs[:, 2 * P:3 * P], v[:, 1, :], False, True)\
                    .then_inc(pv_done, 1)

            def turned(group, n):
                pe.wait_ge(y_ready, 4 * group + (n + 3))
                if n:
                    pe.wait_ge(mix_ready, 4 * group + n)
                for t in range(TT):
                    ins = pe.transpose(bank[:, B_T, t * P:(t + 1) * P], y[:, n % 2, t, :], ident)
                ins.then_inc(yT_done, 1)

            def gate_units(group, rnd, event):
                def before(s):
                    if s % 2 == 0:
                        scores(group, s // 2)

                def after(s):
                    if s % 2 == 1:
                        weighted(group, s // 2)
                        if s >= 5:
                            turned(group, (s - 5) // 2)

                for u in range(2):
                    unit_columns(rnd, u, event + u, hT, before, after)

            def left_over(group):
                return lambda s: turned(group, 2 + s // 2) if s in (1, 3) else None

            unit_columns(R_IN, 0, event_of(R_IN, 0), hT)
            unit_columns(R_IN, 1, event_of(R_IN, 1), hT,
                         after=lambda s: gate_columns() if s == 6 else None)
            for u in range(2):
                unit_columns(R_IN + 1, u, event_of(R_IN + 1, u), hT,
                             after=lambda s: spread_rows() if s == 0 else None)
            with pe.Fori(0, 3) as j:
                gate_units(j, 3 * j + gate_round(0), 6 * j + event_of(gate_round(0), 0))
                for n in (1, 2):
                    for u in range(2):
                        unit_columns(3 * j + (gate_round(0) + n), u,
                                     6 * j + event_of(gate_round(0) + n, u), hT,
                                     after=left_over(j) if n == 1 else None)
            gate_units(3, gate_round(3), event_of(gate_round(3), 0))

            for g in range(4):
                pe.wait_ge(acc_free, E_OUT + g + 1)
                for s in range(8 if g < 3 else 8 - SPLIT_OUT):
                    if g == 0:
                        pe.wait_ge(mix_lo, 2 * s + 2)
                    sub_tokens(8 * (R_OUT + g) + s + 1, s % AHEAD, mixT, g % 2, 2 * s, KT - 1)
                    if g == 0:
                        left_over(3)(s)
            last_subs(8 * (R_OUT + 3), 8 - SPLIT_OUT, 8, mixT, 1)

            def chunk_transposed(c):
                for t in range(TT):
                    pe.wait_ge(resid_ready, ((1, 3), (3, 4), (5, 6), (7, 8))[c][t])
                    for b in (2 * c, 2 * c + 1):
                        transposed(resid, t, b)

            def first_pair(s):
                if s < 4:
                    pe.wait_ge(xT_lo, KT + 4 * (s + 1))

            def first_pair_after(s):
                if s < 2:
                    chunk_transposed(s + 2)
                if s == 5:
                    pe.wait_ge(h_ready, CHUNKS * TT + TT)
                    for t in range(TT):
                        ins = mm(bank[:, B_S, t * P:(t + 1) * P], ff_u[:, 0, t * P:(t + 1) * P], ident,
                                 True, True)
                    ins.then_inc(rms_spread, 1)

            keep_clock(14, 7)
            chunk_transposed(0)
            chunk_transposed(1)
            for u in range(2):
                unit_columns(R_FF, u, E_FF + u, h2T, first_pair, first_pair_after)
            with pe.Fori(1, PAIRS) as i:
                for u in range(2):
                    unit_columns(i + R_FF, u, 2 * i + (E_FF + u), h2T)

            for g in range(4):
                pe.wait_ge(acc_free, E_DOWN + g + 1)
                for s in range(DOWN_SUBS if g < 3 else DOWN_SUBS - AHEAD):
                    n = DOWN_SUBS * g + s
                    if g == 0:
                        pe.wait_ge(ff_lo, s + 1)
                    sub_tokens(8 * R_DOWN + n + 1, n % AHEAD, ffT, g % 2, 2 * s, KF - 1)
            last_subs(8 * R_DOWN + 3 * DOWN_SUBS, DOWN_SUBS - AHEAD, DOWN_SUBS, ffT, 1)


_INS = ["x", "positions", "g_mix_pre", "w_in", "conv_w", "conv_b", "b_igate", "b_fgate",
        "g_mlstm_head", "g_ret_head", "w_out", "g_mix_post", "g_ffn_pre", "w_gate", "w_up", "w_down",
        "g_ffn_post"]


def kernel(**inputs):
    import concourse.bacc as bacc
    from concourse.bass_utils import run_bass_kernel_spmd

    nc = bacc.Bacc("TRN2", target_bir_lowering=False, num_devices=1)
    arrays, args = {}, []
    steps = np.arange(0, HD, 2, dtype=np.float32) / np.float32(HD)
    inv_freq = np.power(np.float32(10000.0), -steps).astype(np.float32)
    constants = {"inv_freq": np.concatenate([inv_freq, inv_freq]).reshape(P, 1)}
    for name in _INS + ["inv_freq"]:
        a = np.ascontiguousarray(constants[name] if name in constants else inputs[name])
        if a.ndim == 3 and a.shape[0] == 1 and name.startswith("w_"):
            a = a[0]
        arrays[f"in_{name}"] = a
        args.append(nc.dram_tensor(f"in_{name}", a.shape, mybir.dt.from_np(a.dtype),
                                   kind="ExternalInput").ap())
    out = nc.dram_tensor("out_0", (1, SEQ, D), F32, kind="ExternalOutput").ap()
    hybrid_layer(nc, *args, out)
    r = run_bass_kernel_spmd(nc, [arrays], core_ids=[0])
    return r.results[0]["out_0"]
```
